# Optimizing a Trainium2 kernel written in Bass

```python
import jax, jax.numpy as jnp
from jax import lax
import numpy as np

D_MODEL = 2048
BATCH = 1
SEQ = 512
DEPTH = 1
DEC_BATCH = 8
DEC_SEQ = 8
PAST_LEN = 256
PAGE_SIZE = 128

N_HEADS = 16
N_KV = 4
GROUP = N_HEADS // N_KV
HEAD_DIM = D_MODEL // 32
NSA_WIDTH = N_HEADS * HEAD_DIM
BLK = 64
CMP_HIDDEN = 2 * HEAD_DIM
TOP_N = 16
WINDOW = 512
Q_BLOCK = 128
POOL_WINDOWS = (2, 4, 8, 16)
POOL_GROUPS = 4
POOL_WIDTH = D_MODEL // 2
POOL_GW = POOL_WIDTH // POOL_GROUPS
POOL_STATE = max(POOL_WINDOWS) - 1
D_FF = 4 * D_MODEL
EPS = 1e-6
NEG = -1e30
FORCED = 1e4

KV_COLS = 2 * N_KV * HEAD_DIM
SPLIT_SIZES = (NSA_WIDTH, KV_COLS, KV_COLS, KV_COLS, 3 * N_HEADS, POOL_WIDTH, 2 * D_MODEL)
IN_COLS = sum(SPLIT_SIZES)
SPLITS = tuple(int(v) for v in np.cumsum(SPLIT_SIZES)[:-1])

kernel_name = 'nsa_pool_gated_hybrid_step'

F32 = jnp.float32

def rmsnorm(x, g):
    xf = x.astype(F32)
    y = xf * lax.rsqrt(jnp.mean(xf * xf, axis=-1, keepdims=True) + EPS)
    return (y * g.astype(F32)).astype(x.dtype)

def project_in(x, g, w):
    n, T, _ = x.shape
    z = rmsnorm(x, g) @ w
    q, kc, ks, kw, ng, u, mg = jnp.split(z, SPLITS, axis=-1)
    q = q.reshape(n, T, N_KV, GROUP, HEAD_DIM)
    kv = lambda a: a.reshape(n, T, 2, N_KV, HEAD_DIM)
    ng = jnp.moveaxis(jax.nn.sigmoid(ng.astype(F32)).reshape(n, T, 3, N_KV, GROUP), 2, -1).astype(x.dtype)
    mg = jax.nn.sigmoid(mg.astype(F32)).reshape(n, T, 2, D_MODEL).astype(x.dtype)
    return q, kv(kc), kv(ks), kv(kw), ng, u, mg

def compress(rows, pe, w1, w2):
    n, L = rows.shape[:2]
    nb = L // BLK
    blk = rows.reshape(n, nb, BLK, N_KV, HEAD_DIM) + pe[None, None, :, None, :]
    flat = blk.transpose(0, 1, 3, 2, 4).reshape(n, nb, N_KV, BLK * HEAD_DIM)
    return jax.nn.gelu(flat @ w1) @ w2

def nsa_core(q, q_pos, k_cmp, v_cmp, k_sel, v_sel, k_win, v_win, win_pos, gate):
    scale = HEAD_DIM ** -0.5
    nb = k_cmp.shape[1]
    bidx = jnp.arange(nb)
    qp = q_pos[:, None]
    cmask = (bidx * BLK + BLK - 1)[None, :] <= qp
    s = jnp.einsum('nqhgd,nbhd->nhgqb', q, k_cmp, preferred_element_type=F32) * scale
    p = jnp.where(cmask, jax.nn.softmax(jnp.where(cmask, s, NEG), axis=-1), 0.0)
    o_cmp = jnp.einsum('nhgqb,nbhd->nqhgd', p.astype(v_cmp.dtype), v_cmp)
    cur = qp // BLK
    forced = (bidx == 0) | (bidx == cur) | (bidx == cur - 1)
    cand = bidx * BLK <= qp
    score = jnp.where(cand, jnp.where(forced, FORCED, p.sum(axis=2)), NEG)
    top_s, top_i = lax.top_k(score, min(TOP_N, nb))
    gather = jax.vmap(jax.vmap(lambda a, i: a[i]))
    gk = gather(k_sel, top_i)
    gv = gather(v_sel, top_i)
    kpos = top_i[..., None] * BLK + jnp.arange(BLK)
    smask = (top_s > NEG / 2)[..., None] & (kpos <= q_pos[:, None, None])
    s2 = jnp.einsum('nqhgd,nhqkbd->nhgqkb', q, gk, preferred_element_type=F32) * scale
    s2 = jnp.where(smask[:, :, None], s2, NEG)
    sh = s2.shape
    p2 = jax.nn.softmax(s2.reshape(sh[:4] + (-1,)), axis=-1).reshape(sh)
    o_sel = jnp.einsum('nhgqkb,nhqkbd->nqhgd', p2.astype(gv.dtype), gv)
    wp = win_pos[None, :]
    wmask = (wp <= qp) & (wp >= qp - WINDOW) & (wp >= 0)
    s3 = jnp.einsum('nqhgd,nshd->nhgqs', q, k_win, preferred_element_type=F32) * scale
    p3 = jax.nn.softmax(jnp.where(wmask, s3, NEG), axis=-1)
    o_win = jnp.einsum('nhgqs,nshd->nqhgd', p3.astype(v_win.dtype), v_win)
    g = gate.astype(o_cmp.dtype)
    o = g[..., 0:1] * o_cmp + g[..., 1:2] * o_sel + g[..., 2:3] * o_win
    return o.reshape(o.shape[:2] + (NSA_WIDTH,))

def nsa_prompt(q, kvc, kvs, kvw, gate, cw, cv):
    n, T = q.shape[:2]
    nb = T // BLK
    k_cmp = compress(kvc[:, :, 0], *cw)
    v_cmp = compress(kvc[:, :, 1], *cv)
    sel = kvs.reshape(n, nb, BLK, 2, N_KV, HEAD_DIM).transpose(3, 0, 4, 1, 2, 5)
    nqb = T // Q_BLOCK
    kw = jnp.pad(kvw, ((0, 0), (WINDOW, 0), (0, 0), (0, 0), (0, 0)))
    widx = jnp.arange(nqb)[:, None] * Q_BLOCK + jnp.arange(WINDOW + Q_BLOCK)[None, :]
    wblk = jnp.moveaxis(kw[:, widx], 1, 0)
    wpos = widx - WINDOW
    qb = jnp.moveaxis(q.reshape(n, nqb, Q_BLOCK, N_KV, GROUP, HEAD_DIM), 1, 0)
    gb = jnp.moveaxis(gate.reshape(n, nqb, Q_BLOCK, N_KV, GROUP, 3), 1, 0)
    pos = jnp.arange(T).reshape(nqb, Q_BLOCK)

    def step(args):
        qi, gi, wi, wpi, pi = args
        return nsa_core(qi, pi, k_cmp, v_cmp, sel[0], sel[1], wi[:, :, 0], wi[:, :, 1], wpi, gi)

    out = lax.map(step, (qb, gb, wblk, wpos, pos))
    return jnp.moveaxis(out, 0, 1).reshape(n, T, NSA_WIDTH)

def nsa_sample(q, kvc, kvs, kvw, gate, cache_cmp, cache_sel, cache_win, page_table, cw, cv):
    n, T = q.shape[:2]
    L = PAST_LEN + T
    Lp = -(-L // BLK) * BLK

    def full_rows(cache, new):
        past = cache[page_table].reshape(n, PAST_LEN, 2, N_KV, HEAD_DIM)
        rows = jnp.concatenate([past, new], axis=1)
        return jnp.pad(rows, ((0, 0), (0, Lp - L), (0, 0), (0, 0), (0, 0)))

    rc = full_rows(cache_cmp, kvc)
    k_cmp = compress(rc[:, :, 0], *cw)
    v_cmp = compress(rc[:, :, 1], *cv)
    rs = full_rows(cache_sel, kvs)
    sel = rs.reshape(n, Lp // BLK, BLK, 2, N_KV, HEAD_DIM).transpose(3, 0, 4, 1, 2, 5)
    wrows = jnp.concatenate([cache_win, kvw], axis=1)
    wb = cache_win.shape[1]
    wpos = PAST_LEN - wb + jnp.arange(wb + T)
    pos = PAST_LEN + jnp.arange(T)
    qs = jnp.moveaxis(q, 1, 0)[:, :, None]
    gs = jnp.moveaxis(gate, 1, 0)[:, :, None]

    def step(args):
        qi, gi, pi = args
        return nsa_core(qi, pi[None], k_cmp, v_cmp, sel[0], sel[1], wrows[:, :, 0], wrows[:, :, 1], wpos, gi)

    out = lax.map(step, (qs, gs, pos))
    new_win = wrows[:, -min(WINDOW, wb + T):]
    return jnp.moveaxis(out[:, :, 0], 0, 1), new_win

def pool_mix(u, past, w_grp, scale):
    n, T, _ = u.shape
    xx = u if past is None else jnp.concatenate([past, u], axis=1)
    P = xx.shape[1] - T
    cs = jnp.pad(jnp.cumsum(xx.astype(F32), axis=1), ((0, 0), (1, 0), (0, 0)))
    end = P + jnp.arange(T) + 1
    uf = u.astype(F32)
    outs = []
    for gi, w in enumerate(POOL_WINDOWS):
        c0, c1 = gi * POOL_GW, (gi + 1) * POOL_GW
        start = jnp.maximum(end - w, 0)
        cnt = (end - start).astype(F32)[None, :, None]
        cg = cs[:, :, c0:c1]
        outs.append((cg[:, end] - cg[:, start]) / cnt - uf[..., c0:c1])
    d = jnp.stack(outs, axis=2).astype(u.dtype)
    y = jnp.einsum('ntgc,gce->ntge', d, w_grp).reshape(n, T, POOL_WIDTH) * scale
    return y, xx[:, -POOL_STATE:]

def merge_and_mlp(x, o_nsa, o_pool, mg, w_br_nsa, w_br_pool, w_o, g_mlp, w_up, w_down):
    m = mg[:, :, 0] * (o_nsa @ w_br_nsa) + mg[:, :, 1] * (o_pool @ w_br_pool)
    x = x + m @ w_o
    h = rmsnorm(x, g_mlp)
    return x + jnp.square(jax.nn.relu(h @ w_up)) @ w_down

def setup_inputs(seed: int = 0) -> dict:
    key = jax.random.key(seed)
    ks = jax.random.split(key, 32)
    nrm = lambda k, shape, fan: jax.random.normal(k, shape, F32) * fan ** -0.5
    rnd = lambda k, shape: jax.random.normal(k, shape, F32)
    n_pages = PAST_LEN // PAGE_SIZE
    n_used = DEC_BATCH * n_pages
    n_phys = n_used + max(1, n_used // 4)
    wb = min(WINDOW, PAST_LEN)
    page_table = jax.random.permutation(ks[6], n_phys)[:n_used].reshape(DEC_BATCH, n_pages).astype(jnp.int32)
    return {
        'x_prompt': rnd(ks[0], (BATCH, SEQ, D_MODEL)),
        'x_sample': rnd(ks[1], (DEC_BATCH, DEC_SEQ, D_MODEL)),
        'cache_cmp_kv': rnd(ks[2], (DEPTH, n_phys, PAGE_SIZE, 2, N_KV, HEAD_DIM)),
        'cache_sel_kv': rnd(ks[3], (DEPTH, n_phys, PAGE_SIZE, 2, N_KV, HEAD_DIM)),
        'cache_win_kv': rnd(ks[4], (DEPTH, DEC_BATCH, wb, 2, N_KV, HEAD_DIM)),
        'state_pool': rnd(ks[5], (DEPTH, DEC_BATCH, POOL_STATE, POOL_WIDTH)),
        'page_table': page_table,
        'g_mix': 1.0 + 0.1 * rnd(ks[7], (DEPTH, D_MODEL)),
        'w_in': nrm(ks[8], (DEPTH, D_MODEL, IN_COLS), D_MODEL),
        'pe_ck': 0.1 * rnd(ks[9], (DEPTH, BLK, HEAD_DIM)),
        'w_ck1': nrm(ks[10], (DEPTH, BLK * HEAD_DIM, CMP_HIDDEN), BLK * HEAD_DIM),
        'w_ck2': nrm(ks[11], (DEPTH, CMP_HIDDEN, HEAD_DIM), CMP_HIDDEN),
        'pe_cv': 0.1 * rnd(ks[12], (DEPTH, BLK, HEAD_DIM)),
        'w_cv1': nrm(ks[13], (DEPTH, BLK * HEAD_DIM, CMP_HIDDEN), BLK * HEAD_DIM),
        'w_cv2': nrm(ks[14], (DEPTH, CMP_HIDDEN, HEAD_DIM), CMP_HIDDEN),
        'w_pool_grp': nrm(ks[15], (DEPTH, POOL_GROUPS, POOL_GW, POOL_GW), POOL_GW),
        'pool_scale': 1.0 + 0.1 * rnd(ks[16], (DEPTH, POOL_WIDTH)),
        'w_br_nsa': nrm(ks[17], (DEPTH, NSA_WIDTH, D_MODEL), NSA_WIDTH),
        'w_br_pool': nrm(ks[18], (DEPTH, POOL_WIDTH, D_MODEL), POOL_WIDTH),
        'w_o': nrm(ks[19], (DEPTH, D_MODEL, D_MODEL), D_MODEL),
        'g_mlp': 1.0 + 0.1 * rnd(ks[20], (DEPTH, D_MODEL)),
        'w_up': nrm(ks[21], (DEPTH, D_MODEL, D_FF), D_MODEL),
        'w_down': nrm(ks[22], (DEPTH, D_FF, D_MODEL), D_FF),
        'g_final': 1.0 + 0.1 * rnd(ks[23], (D_MODEL,)),
    }

def reference(x_prompt, x_sample, cache_cmp_kv, cache_sel_kv, cache_win_kv, state_pool, page_table,
              g_mix, w_in, pe_ck, w_ck1, w_ck2, pe_cv, w_cv1, w_cv2, w_pool_grp, pool_scale,
              w_br_nsa, w_br_pool, w_o, g_mlp, w_up, w_down, g_final):
    xp, xs = x_prompt, x_sample
    p_cmp, p_sel, p_win, p_pool = [], [], [], []
    s_cmp, s_sel, s_win, s_pool = [], [], [], []
    for l in range(DEPTH):
        cw = (pe_ck[l], w_ck1[l], w_ck2[l])
        cv = (pe_cv[l], w_cv1[l], w_cv2[l])
        tail = (w_br_nsa[l], w_br_pool[l], w_o[l], g_mlp[l], w_up[l], w_down[l])
        q, kvc, kvs, kvw, ng, u, mg = project_in(xp, g_mix[l], w_in[l])
        o_nsa = nsa_prompt(q, kvc, kvs, kvw, ng, cw, cv)
        o_pool, pst = pool_mix(u, None, w_pool_grp[l], pool_scale[l])
        xp = merge_and_mlp(xp, o_nsa, o_pool, mg, *tail)
        p_cmp.append(kvc)
        p_sel.append(kvs)
        p_win.append(kvw[:, -min(WINDOW, kvw.shape[1]):])
        p_pool.append(pst)
        q, kvc, kvs, kvw, ng, u, mg = project_in(xs, g_mix[l], w_in[l])
        o_nsa, new_win = nsa_sample(q, kvc, kvs, kvw, ng, cache_cmp_kv[l], cache_sel_kv[l],
                                    cache_win_kv[l], page_table, cw, cv)
        o_pool, sst = pool_mix(u, state_pool[l], w_pool_grp[l], pool_scale[l])
        xs = merge_and_mlp(xs, o_nsa, o_pool, mg, *tail)
        s_cmp.append(kvc)
        s_sel.append(kvs)
        s_win.append(new_win)
        s_pool.append(sst)
    y_prompt = rmsnorm(xp, g_final)
    y_sample = rmsnorm(xs, g_final)
    return (y_prompt, y_sample, jnp.stack(p_cmp), jnp.stack(p_sel), jnp.stack(p_win), jnp.stack(p_pool),
            jnp.stack(s_cmp), jnp.stack(s_sel), jnp.stack(s_win), jnp.stack(s_pool))


_drawn_inputs = setup_inputs


def setup_inputs(seed=0):
    import zlib

    import numpy as np

    out = dict(_drawn_inputs(seed))
    spreads = {}
    factors = {'pe_ck': 21.364, 'pe_cv': 3.486}
    for name, (base, spread) in spreads.items():
        noise = np.random.default_rng([zlib.crc32(name.encode()), seed]).standard_normal(out[name].shape)
        drawn = base * np.exp(spread * noise) if base else spread * noise
        out[name] = __import__('jax').numpy.asarray(drawn.astype(out[name].dtype))
    for name, factor in factors.items():
        out[name] = (out[name] * factor).astype(out[name].dtype)
    return out
```

```python
from contextlib import ExitStack

import concourse.bass as bass
from concourse import mybir

F32 = mybir.dt.float32
F32R = mybir.dt.float32r
BF16 = mybir.dt.bfloat16
I32 = mybir.dt.int32
ALU = mybir.AluOpType
ACT = mybir.ActivationFunctionType
X = mybir.AxisListType.X

P = 128
D = 2048
KT = D // P
SEQ = 512
NB = 8
NT = 8
NS = NB * NT
TOK = SEQ + NS
HALF = TOK // 2
TT = 5
HEADS, NKV, HD = 16, 4, 64
PAST, PAGE, BLK = 256, 128, 64
PAGES = PAST // PAGE
KEYS = PAST + NT
KVC = 2 * NKV * HD
PW = 1024
PSTATE = 15
FF = 4 * D
EPS = 1e-6
NEG = -1e30
Q_COL, KV_COL, NG_COL, U_COL = 0, 1024, 1024 + 3 * KVC, 1024 + 3 * KVC + 3 * HEADS
MG_COL = U_COL + PW

C_U = 0
C_KV = C_U + 8
C_NG = C_KV + 12
C_PM = C_NG + 1
C_Q = C_PM + 1
C_MG = C_Q + 8
C_BR = C_MG + 32
C_WO = C_BR + 16
C_FF = C_WO + 16
A_X = 0
A_U = A_X + KT
A_KV = A_U + 8
A_PM = A_KV + 12
A_Q = A_PM + 8
A_MG = A_Q + 8
A_BR = A_MG + 32
A_WO = A_BR + 16
A_FF = A_WO + 16
FFG = 8
GK = FF // FFG // P
UP_PAIRS, DOWN_PAIRS = GK // 2, 4
C_GROUP = GK + 8
A_GROUP = GK + KT


def build(nc, x_prompt, x_sample, cache_cmp, cache_sel, cache_win, state_pool, page_table,
          g_mix, w_in, pe_ck, w_ck1, w_ck2, pe_cv, w_cv1, w_cv2, w_pool, pool_scale,
          w_nsa, w_bpool, w_o, g_mlp, w_up, w_down, g_final,
          y_p, y_s, p_cmp, p_sel, p_win, p_pool, s_cmp, s_sel, s_win, s_pool):
    def dram(name, shape):
        return nc.dram_tensor(name, shape, F32, kind="Internal").ap()

    qT_d = dram("qT_scratch", [8, P, TOK])
    kvT_d = dram("kvT_scratch", [12, P, TOK])
    kv_d = dram("kv_scratch", [TOK, 3 * KVC])
    gate_d = dram("gate_scratch", [NS, 3 * HEADS])
    mg_d = dram("mg_scratch", [32, P, TOK])
    kc_d = dram("kcmp_scratch", [NKV, HD, 40])
    vc_d = dram("vcmp_scratch", [NKV, 40, HD])

    with ExitStack() as ctx:
        arena = ctx.enter_context(nc.sbuf_tensor("arena", [P, 53200], F32))
        base = (nc.sbuf_base - 53200 * 4) // 32 * 32
        del arena

        def at(name, shape, offset, dt=F32):
            return nc.alloc_sbuf_tensor_at(name, shape, dt, offset=base + offset)

        def sem(name):
            return ctx.enter_context(nc.semaphore(name))

        RX, RM, RW, RE = 0, 73728, 147456, 196608
        A_hi = at("movA_hi", [P, KT, TOK], RX, F32R)
        A_lo = at("movA_lo", [P, KT, TOK], RX + 36864, F32R)
        B_hi = at("movB_hi", [P, KT, TOK], RM, F32R)
        B_lo = at("movB_lo", [P, KT, TOK], RM + 36864, F32R)
        x2T = at("x2T", [P, KT, TOK], RX)
        F_hi = at("ffn_hi", [P, GK, TOK], RX + 36864, F32R)
        F_lo = at("ffn_lo", [P, GK, TOK], RX + 55296, F32R)
        raw = [at(f"raw{s}", [P, KT * P], RW + 8192 * s) for s in range(2)]
        w_hi = [at(f"w_hi{s}", [P, KT * P], RW + 16384 + 16384 * s, F32R) for s in range(2)]
        w_lo = [at(f"w_lo{s}", [P, KT * P], RW + 24576 + 16384 * s, F32R) for s in range(2)]
        xn = at("xn", [P, TT, D], RM)
        junk = at("junk", [P, D], RM + 40960)
        stN = at("stN", [NB * PSTATE, PW], RM + 49152)
        stT = at("stT", [P, 8, NB * PSTATE], RM + 53248)
        uT = at("uT", [P, 8, TOK], RM)
        dT = at("dT", [P, 8, TOK], RM + 18432)
        PADW = 16
        wa = [at(f"win_sum{s}", [P, PADW + SEQ], RM + 57344 + 2112 * s) for s in range(2)]
        sa = [at(f"win_sum_s{s}", [P, NB, PSTATE + NT], RM + 61568 + 736 * s) for s in range(2)]
        D_hi = at("d_hi", [P, 8, TOK], RM + 36864, F32R)
        D_lo = at("d_lo", [P, 8, TOK], RM + 55296, F32R)
        unat = at("unat", [79, PW], RM + 63488)
        oP = at("oP", [P, 8, TOK], RM + 18432)
        oN = at("oN", [P, 8, TOK], RM)
        NROW = 21
        crow = at("crow", [P, NROW, NKV, HD], RM + 36864)
        w1 = [at(f"w1_{s}", [P, 16, P], RM + 8192 * s) for s in range(2)]

        G = at("cmp_hidden", [P, NKV, 20, 2], RM + 16384)
        kcs = at("kcs", [HD, NKV, 40], RM + 17024)
        w2 = [at(f"w2_{j}", [P, HD], RM + 17664 + 256 * j) for j in range(2)]
        peb = at("peb", [P, 1], RM + 18176)
        vcs = at("vcs", [40, NKV, HD], RM + 58368)
        RA = RM + 36864
        KTp = at("KTp", [HD, 2, SEQ], RA)
        Vp = at("Vp", [P, 2, 4, HD], RA + 4096)
        qh = at("qh", [HD, 2, SEQ], RA + 6144)
        kch = at("kch", [HD, 8], RA + 10240)
        vch = at("vch", [8, HD], RA + 10272)
        Pb = [at(f"Pb{j}", [P, 2, SEQ], RA + 10528 + 4096 * j) for j in range(2)]
        PTb = [at(f"PTb{j}", [P, SEQ], RA + 18720 + 2048 * j) for j in range(2)]
        kvp = at("kvp", [P, 2, PAGES, KVC], RA + 22816)
        vnew = at("vnew", [NT, 2, NKV * HD], RA + 31008)
        qz = at("qz", [P, NKV, 4, NT], RA + 33056)
        Ps = at("Ps", [P, 2, KEYS], RA + 33568)
        kc4 = at("kc4", [P, 2, 4], RA + 35680)
        pcs = at("pcs", [P, 4, 8], RA + 35712)
        pcm = at("pcm", [P, 4, 8], RA + 35840)
        pcT = at("pcT", [8, SEQ], RE + 13888)
        pc4 = at("pc4", [P, 4], RA + 35968)
        pcT4 = at("pcT4", [4, P], RA + 36000)
        nmc, rsc, wc = (at(f"cstat{j}", [P, 4], RA + 36512 + 32 * j) for j in range(3))
        nmx, rsx, wx = (at(f"pstat{j}", [P, 2, 2], RA + 36608 + 32 * j) for j in range(3))
        nms, rss, wsm = (at(f"sstat{j}", [P, 4], RA + 36704 + 32 * j) for j in range(3))

        off = [RE]

        def small(name, shape, dt=F32):
            n = 2 if dt == BF16 else 4
            for q in shape[1:]:
                n *= q
            o = off[0]
            off[0] += (n + 31) // 32 * 32
            assert off[0] <= 53200 * 4, name
            return at(name, shape, o, dt)

        ident = small("ident", [P, P])
        identb = small("identb", [P, P], BF16)
        onesm = small("ones", [P, P])
        cmask = small("cmask", [P, P], BF16)
        smask = small("smask", [P, NT], BF16)
        bmask = small("bmask", [P, 4, 8])
        vis = small("vis", [P, 4])
        gmix, gmlp, gfin = (small(n, [P, KT]) for n in ("gmix", "gmlp", "gfin"))
        psc = small("psc", [P, 8])
        gp = small("gp", [P, 4, 3 * HEADS])
        gn = small("gn", [NS, 3 * HEADS])
        gs = small("gs", [P, NB, 3])
        rc = small("rc", [P, 4, 16])
        st5 = [small(f"stat{j}", [P, 8]) for j in range(4)]
        ez = small("ez", [1, 8])
        pt = small("pt", [1, NB * PAGES], I32)
        RT = off[0]
        zT = [small(f"zT{s}", [P, TOK]) for s in range(2)]
        RN = off[0]
        zn = [small(f"zn{s}", [P, TT, P]) for s in range(2)]
        assert RN + 5248 <= RE + 13888
        KTs = at("KTs", [P, 2, 2, KEYS], RN)
        vc4 = at("vc4", [4, NKV, HD], RN + 4224)
        xr = [at(f"xr{s}", [P, TT, P], RN + 2560 * s) for s in range(2)]
        mgl = [at(f"mgl{s}", [P, 2, TOK], RT + 4608 * s) for s in range(2)]
        sq = [at(f"sq{s}", [P, TOK], RT + 2304 * s) for s in range(2)]
        rB = at("rB", [P, TOK], RN)
        tB = at("tB", [P, TOK], RN + 2304)
        ff = [at(f"ff{s}", [P, TOK], RT + 2304 * s) for s in range(2)]
        ff2 = [at(f"ff2_{s}", [P, TOK], RN + 2304 * s) for s in range(2)]
        yT = [at(f"yT{s}", [P, TOK], RM + 2304 * s) for s in range(2)]
        yn = [at(f"yn{s}", [P, TT, P], RM + 8192 + 2560 * s) for s in range(2)]
        rF = at("rF", [P, TOK], RM + 16384)
        tF = at("tF", [P, TOK], RM + 18688)

        PS = ctx.enter_context(nc.psum_tensor("PS", [P, 8, 512], F32))

        def acc(slot, n=2):
            return PS[:, n * slot:n * slot + n, 0:HALF]

        def flat(slot):
            return PS[:, 2 * slot:2 * slot + 2, :].rearrange("p b n -> p (b n)")[:, 0:TT * P]

        def halves(t2d):
            return t2d.rearrange("p (h n) -> p h n", h=2)

        names = """x_loaded0 x_loaded1 x_loaded2 x_loaded3 x_loaded4 small_loaded state_loaded consts_ready
            sq_done rstd_step rc_done stats_set x_scaled x_hi st_ready st_copied
            raw_full0 raw_full1 split_hi split_lo acc_ready acc_free
            zT_stored0 zT_stored1 nat_ready0 nat_ready1 zn_done0 zn_done1 zn_stored0 zn_stored1
            out_stored tail_stored chain_p pooled chain_v chain_a tail_ready
            ng_ready gate_exp gateT_done ng_turned gates_done gn_stored gs_loaded d_high d_ready
            crow_loaded w1_loaded0 w1_loaded1 w1_used w2_loaded pe_out gelu_done kc_out c2_ready c2_done
            kc_stored
            smp_loaded head_loaded smask_built half_full0 half_full1 chain_att br_sum A_split h_ready bank7_free
            KT_ready KT_copied ss_ready smax_done sexp_done sP_ready sPT_ready sPT_copied so_ready
            cs_ready cmask_done cexp_done cP_ready cPT_ready cPT_copied
            s_ready max_done exp_done P_ready PT_ready PT_copied pv_done 
            mg_exp mg_done
            A_high merged x_turned xT_copied mg_loaded0 mg_loaded1 br_high xr_loaded0 xr_loaded1
            sq_ready sq_used ms_ready root_in root_done h_in h_high ff_relu ff_high ff_ready
            yT_in yT_scaled y_turned yn_done yn_stored0 yn_stored1""".split()
        S = {n: sem(n) for n in names}
        raw_full = [S["raw_full0"], S["raw_full1"]]
        SMP_DMAS, HEAD_DMAS = 13, 8
        CHAIN_SMP, CHAIN_HEAD = 3, 13

        w_in_v = w_in[0].rearrange("(k p) n -> p k n", p=P)
        block = ctx.enter_context(nc.Block())

        @block.sync
        def _(sp):
            def load(slot, src):
                sp.dma_start(raw[slot][:].rearrange("p (k n) -> p k n", n=P), src).then_inc(raw_full[slot], 16)

            def load_in(slot, col):
                load(slot, w_in_v[:, :, bass.ds(col, P)])

            for t in range(4):
                sp.dma_start(xn[:, t, :], x_prompt[0, t * P:(t + 1) * P, :]).then_inc(S[f"x_loaded{t}"], 16)
            sp.dma_start(xn[0:NS, 4, :], x_sample.rearrange("b t d -> (b t) d")).then_inc(S["x_loaded4"], 16)
            load_in(0, U_COL)
            load_in(1, U_COL + P)
            with sp.Fori(0, 3) as i:
                for s in range(2):
                    sp.wait_ge(S["split_lo"], C_U + 2 * i + s + 1)
                    load_in(s, U_COL + P * (2 * i + s + 2))
            for s in range(2):
                sp.wait_ge(S["split_lo"], C_U + 6 + s + 1)
                load_in(s, KV_COL + P * s)

            def kv_pair(i, last=False):
                for s in range(2):
                    sp.wait_ge(S["split_lo"], C_KV + 2 * i + s + 1)
                    if last and s == 1:
                        sp.dma_start(raw[s][:].rearrange("p (g c n) -> p g c n", g=4, c=2),
                                     w_pool[0].rearrange("g (c p) n -> p g c n", p=P)).then_inc(raw_full[s], 16)
                    else:
                        load_in(s, KV_COL + P * (2 * i + 2 + s))
                    sp.wait_ge(S["acc_free"], A_KV + 2 * i + s + 1)
                    sp.dma_start(kvT_d[bass.ds(2 * i + s, 1)].rearrange("m p n -> p (m n)"), zT[s][:])\
                        .then_inc(S[f"zT_stored{s}"], 16)
                for s in range(2):
                    col = P * (2 * i + s)
                    sp.wait_ge(S[f"zn_done{s}"], 2 * i + 3)
                    sp.dma_start(kv_d[0:SEQ, bass.ds(col, P)].rearrange("(t p) n -> p t n", p=P), zn[s][:, 0:4, :])\
                        .then_inc(S[f"zn_stored{s}"], 16)
                    sp.dma_start(kv_d[SEQ:TOK, bass.ds(col, P)], zn[s][0:NS, 4, :]).then_inc(S[f"zn_stored{s}"], 16)

            with sp.Fori(0, 5) as i:
                kv_pair(i)
            kv_pair(5, last=True)

            def weights(slot, n, src, dst=None):
                sp.wait_ge(S["split_lo"], n - 1)
                sp.dma_start(raw[slot][:].rearrange("p (k n) -> p k n", n=P) if dst is None else dst, src)\
                    .then_inc(raw_full[slot], 16)

            def halved_weights(s, n, upper, lower):
                sp.wait_ge(S["split_lo"], n - 1)
                w = raw[s][:].rearrange("p (k n) -> p k n", n=P)
                sp.dma_start(w[:, 0:8, :], upper).then_inc(S[f"half_full{s}"], 16)
                sp.dma_start(w[:, 8:16, :], lower).then_inc(raw_full[s], 16)

            for s in range(2):
                weights(s, C_Q + s, w_in_v[:, :, Q_COL + P * s:Q_COL + P * s + P])
            for s in range(2):
                sp.wait_ge(S[f"zn_done{s}"], 1)
            sp.dma_start(p_pool[0, 0], unat[0:PSTATE, :]).then_inc(S["tail_stored"], 16)
            sp.dma_start(s_pool[0, :, PSTATE - NT:PSTATE, :], unat[PSTATE:79, :]).then_inc(S["tail_stored"], 16)
            sp.dma_start(s_pool[0, :, 0:PSTATE - NT, :], state_pool[0, :, NT:PSTATE, :]).then_inc(S["out_stored"], 16)
            for s in range(2):
                sp.wait_ge(S[f"zn_stored{s}"], 32 * 6)
            for r, (po, so) in enumerate(((p_cmp, s_cmp), (p_sel, s_sel), (p_win, None))):
                sp.dma_start(po.rearrange("a b t c h e -> (a b t) (c h e)"), kv_d[0:SEQ, KVC * r:KVC * (r + 1)])\
                    .then_inc(S["out_stored"], 16)
                if so is not None:
                    sp.dma_start(so.rearrange("a b t c h e -> (a b t) (c h e)"), kv_d[SEQ:TOK, KVC * r:KVC * (r + 1)])\
                        .then_inc(S["out_stored"], 16)
            sw = s_win[0].rearrange("b t c h e -> b t (c h e)")
            sp.dma_start(sw[:, 0:PAST, :], cache_win[0].rearrange("b t c h e -> b t (c h e)"))\
                .then_inc(S["out_stored"], 16)
            sp.dma_start(sw[:, PAST:KEYS, :], kv_d[SEQ:TOK, 2 * KVC:].rearrange("(b t) n -> b t n", t=NT))\
                .then_inc(S["out_stored"], 16)
            def gate_weights(s, j):
                col = bass.ds(MG_COL + P * j, P)
                halved_weights(s, C_MG + j, w_in_v[:, 0:8, col], w_in_v[:, 8:16, col])

            def q_pair(i, last=False):
                for s in range(2):
                    if last:
                        gate_weights(s, s)
                    else:
                        weights(s, C_Q + 2 * i + s + 2, w_in_v[:, :, bass.ds(Q_COL + P * (2 * i + s + 2), P)])
                    sp.wait_ge(S["acc_free"], A_Q + 2 * i + s + 1)
                    sp.dma_start(qT_d[bass.ds(2 * i + s, 1)].rearrange("m p n -> p (m n)"), zT[s][:])\
                        .then_inc(S[f"zT_stored{s}"], 16)

            with sp.Fori(0, 3) as i:
                q_pair(i)
            q_pair(3, last=True)
            sp.wait_ge(S["gates_done"], 1)
            sp.dma_start(gate_d, gn[:]).then_inc(S["gn_stored"], 16)
            sp.wait_ge(S["gn_stored"], 16)
            for r in range(3):
                for n in range(HEADS):
                    sp.dma_start(gs[NT * n:NT * n + NT, :, r], gate_d[:, 16 * r + n].rearrange("(b t) -> t b", t=NT),
                                 allow_slow_non_contiguous=True).then_inc(S["gs_loaded"], 16)

            nsa_v = w_nsa[0].rearrange("(k p) n -> p k n", p=P)
            bpool_v = w_bpool[0].rearrange("(k p) n -> p k n", p=P)

            def branch_weights(s, j):
                col = bass.ds(P * j, P)
                halved_weights(s, C_BR + j, nsa_v[:, :, col], bpool_v[:, :, col])

            def mg_pair(i, last=False):
                for s in range(2):
                    if last:
                        branch_weights(s, s)
                    else:
                        gate_weights(s, 2 * i + s + 2)
                for s in range(2):
                    sp.wait_ge(S["mg_done"], 2 * i + s + 1)
                    sp.dma_start(mg_d[bass.ds(2 * i + s, 1)].rearrange("m p n -> p (m n)"), zT[s][:])\
                        .then_inc(S[f"zT_stored{s}"], 16)

            with sp.Fori(0, 15) as i:
                mg_pair(i)
            mg_pair(15, last=True)
            with sp.Fori(0, 7) as i:
                for s in range(2):
                    branch_weights(s, 2 * i + s + 2)
            wo_v = w_o[0].rearrange("(k p) n -> p k n", p=P)
            with sp.Fori(0, 8) as i:
                for s in range(2):
                    weights(s, C_WO + 2 * i + s, wo_v[:, :, bass.ds(P * (2 * i + s), P)])
            up_v = w_up[0].rearrange("(k p) n -> p k n", p=P)
            down_v = w_down[0].rearrange("(g k p) n -> p g k n", p=P, k=GK)
            with sp.Fori(0, FFG) as g:
                with sp.Fori(0, UP_PAIRS) as i:
                    for s in range(2):
                        weights(s, C_FF + C_GROUP * g + 2 * i + s, up_v[:, :, bass.ds(GK * P * g + P * (2 * i + s), P)])
                with sp.Fori(0, DOWN_PAIRS) as i:
                    for s in range(2):
                        weights(s, C_FF + GK + C_GROUP * g + 2 * i + s,
                                down_v[:, bass.ds(g, 1), :, bass.ds(256 * (2 * i + s), 256)]
                                .rearrange("p g k n -> p (g k) n"),
                                raw[s][:].rearrange("p (k n) -> p k n", n=256))
            def y_pair(i):
                for s in range(2):
                    sp.wait_ge(S["yn_done"], 4 * i + 2 * s + 2)
                    col = bass.ds(P * (2 * i + s), P)
                    sp.dma_start(y_p[0].rearrange("(t p) n -> p t n", p=P)[:, :, col], yn[s][:, 0:4, :])\
                        .then_inc(S[f"yn_stored{s}"], 16)
                    sp.dma_start(y_s.rearrange("b t n -> (b t) n")[:, col], yn[s][0:NS, 4, :])\
                        .then_inc(S[f"yn_stored{s}"], 16)

            with sp.Fori(0, 8) as i:
                y_pair(i)
            for s in range(2):
                sp.wait_ge(S[f"yn_stored{s}"], 32 * 8)
            sp.wait_ge(S["out_stored"], 16 * 8)

        @block.gpsimd
        def _(pool):
            n = [0]

            def seq(ins):
                n[0] += 1
                ins.then_inc(S["chain_p"], 1)
                pool.wait_ge(S["chain_p"], n[0])

            for src, dst in ((g_mix, gmix), (g_mlp, gmlp)):
                pool.dma_start(dst[:], src[0].rearrange("(k p) -> p k", p=P),
                               allow_slow_non_contiguous=True).then_inc(S["small_loaded"], 16)
            pool.dma_start(gfin[:], g_final.rearrange("(k p) -> p k", p=P),
                               allow_slow_non_contiguous=True).then_inc(S["small_loaded"], 16)
            pool.dma_start(psc[:], pool_scale[0].rearrange("(k p) -> p k", p=P),
                               allow_slow_non_contiguous=True).then_inc(S["small_loaded"], 16)
            pool.dma_start(pt[:], page_table.rearrange("b n -> (b n)").unsqueeze(0),
                               allow_slow_non_contiguous=True).then_inc(S["small_loaded"], 16)
            pool.dma_start(stN[:], state_pool[0].rearrange("b r c -> (b r) c")).then_inc(S["state_loaded"], 16)
            for st in st5:
                ins = pool.memset(st[:], 1.0)
            ins.then_inc(S["stats_set"], 1)
            seq(pool.memset(ident[:], 0.0))
            seq(pool.affine_select(out=ident[:], in_=ident[:], compare_op=ALU.not_equal, fill=1.0, base=0,
                                   pattern=[[-1, P]], channel_multiplier=1))
            seq(pool.memset(identb[:], 0.0))
            seq(pool.affine_select(out=identb[:], in_=identb[:], compare_op=ALU.not_equal, fill=1.0, base=0,
                                   pattern=[[-1, P]], channel_multiplier=1))
            seq(pool.memset(onesm[:], 1.0))
            seq(pool.memset(cmask[:], 0.0))
            seq(pool.affine_select(out=cmask[:], in_=cmask[:], compare_op=ALU.is_ge, fill=NEG, base=0,
                                   pattern=[[-1, P]], channel_multiplier=1))
            seq(pool.memset(bmask[:], 0.0))
            seq(pool.affine_select(out=bmask[:], in_=bmask[:], compare_op=ALU.is_ge, fill=NEG, base=-(BLK - 1),
                                   pattern=[[P, 4], [-BLK, 8]], channel_multiplier=1))
            seq(pool.memset(vis[:], 1.0))
            seq(pool.affine_select(out=vis[:], in_=vis[:], compare_op=ALU.is_ge, fill=0.0, base=-(BLK - 1),
                                   pattern=[[P, 4]], channel_multiplier=1))
            for t in range(16):
                ins = pool.memset(rc[:, 0, t:t + 1], float(t + 1))
            seq(ins)
            for g in (3, 2, 1):
                seq(pool.tensor_scalar(rc[:, g, :], rc[:, 0, :], float(2 << g), None, ALU.min))
            seq(pool.tensor_scalar(rc[:, 0, :], rc[:, 0, :], 2.0, None, ALU.min))
            for w in wa:
                seq(pool.memset(w[:, 0:PADW], 0.0))
            for j in range(HEADS):
                pool.dma_start(smask[NT * j:NT * j + NT], cmask[0:NT, 0:NT]).then_inc(S["smask_built"], 16)
            pool.wait_ge(S["smask_built"], 16 * HEADS)
            pool.memset(ez[:], 0.0).then_inc(S["consts_ready"], 1)

            pool.wait_ge(S["st_copied"], 1)
            pool.wait_ge(S["rc_done"], 1)
            for m in range(8):
                g = m // 2
                pool.wait_ge(S["acc_free"], A_U + m + 1)
                us = uT[:, m, SEQ:TOK].rearrange("p (b t) -> p b t", t=NT)
                pool.tensor_copy(wa[0][:, PADW:], uT[:, m, 0:SEQ])
                pool.tensor_copy(sa[0][:, :, 0:PSTATE], stT[:, m, :].rearrange("p (b r) -> p b r", r=PSTATE))
                seq(pool.tensor_copy(sa[0][:, :, PSTATE:], us))
                for k in range(g + 1):
                    a, b, sh = k % 2, 1 - k % 2, 1 << k
                    lo = 2 * sh - 1
                    pool.tensor_tensor(wa[b][:, PADW:], wa[a][:, PADW:], wa[a][:, PADW - sh:PADW + SEQ - sh], ALU.add)
                    seq(pool.tensor_tensor(sa[b][:, :, lo:], sa[a][:, :, lo:], sa[a][:, :, lo - sh:PSTATE + NT - sh],
                                           ALU.add))
                r = (g + 1) % 2
                iw = 1.0 / (2 << g)
                pool.tensor_tensor(wa[1 - r][:, PADW:PADW + 16], wa[r][:, PADW:PADW + 16], rc[:, g, :], ALU.mult)
                pool.tensor_scalar(wa[1 - r][:, PADW + 16:], wa[r][:, PADW + 16:], iw, None, ALU.mult)
                seq(pool.tensor_scalar(sa[1 - r][:, :, PSTATE:], sa[r][:, :, PSTATE:], iw, None, ALU.mult))
                pool.tensor_tensor(dT[:, m, 0:SEQ], wa[1 - r][:, PADW:], uT[:, m, 0:SEQ], ALU.subtract)
                pool.tensor_tensor(dT[:, m, SEQ:TOK].rearrange("p (b t) -> p b t", t=NT), sa[1 - r][:, :, PSTATE:], us,
                                   ALU.subtract).then_inc(S["pooled"], 1)
                pool.wait_ge(S["pooled"], m + 1)

            w1c = [w[0].rearrange("(s d) n -> s d n", d=HD) for w in (w_ck1, w_cv1)]
            pool.wait_ge(S["tail_ready"], 1)
            pool.dma_start(w2[0][:], w_ck2[0]).then_inc(S["w2_loaded"], 16)
            pool.dma_start(w2[1][:], w_cv2[0]).then_inc(S["w2_loaded"], 16)

            def w1_load(c):
                s, kv, q = c % 2, c // 4, c % 4
                if c >= 2:
                    pool.wait_ge(S["w1_used"], c - 1)
                for h in range(2):
                    pool.dma_start(w1[s][64 * h:64 * h + 64], w1c[kv][:, 16 * q:16 * q + 16, :])\
                        .then_inc(S[f"w1_loaded{s}"], 16)

            w1_load(0)
            w1_load(1)
            for kv, pe_ in enumerate((pe_ck, pe_cv)):
                if kv == 0:
                    pool.wait_ge(S["acc_ready"], A_PM + 8)
                    for s in range(2):
                        pool.wait_ge(S[f"zn_stored{s}"], 32 * 6)
                else:
                    pool.wait_ge(S["w1_used"], 4)
                cols = slice(4 * HD * kv, 4 * HD * kv + 4 * HD)
                pool.dma_start(crow[:, 0:4].rearrange("p t h e -> p t (h e)"),
                               kv_d[0:SEQ, cols].rearrange("(t p) n -> p t n", p=P)).then_inc(S["crow_loaded"], 16)
                pool.dma_start(crow[0:BLK, 20, 0, :], pe_[0]).then_inc(S["crow_loaded"], 16)
                with pool.Fori(0, NB * PAGES) as j:
                    page = pool.value_load(pt[0:1, bass.ds(j, 1)], min_val=0, max_val=cache_cmp.shape[1] - 1)
                    pool.dma_start(crow[:, bass.ds(4 + j, 1)].rearrange("p t h e -> p (t h e)"),
                                   cache_cmp[0][bass.ds(page, 1), :, kv].rearrange("g s h e -> s (g h e)"))\
                        .then_inc(S["crow_loaded"], 16)
                for c in range(4 * kv + 2, min(4 * kv + 6, 8)):
                    w1_load(c)

            pool.wait_ge(S["c2_done"], 1)
            pool.dma_start(kc_d.rearrange("h e b -> e h b"), kcs[:]).then_inc(S["kc_stored"], 16)
            pool.wait_ge(S["c2_done"], 2)
            pool.dma_start(vc_d.rearrange("h b e -> b h e"), vcs[:]).then_inc(S["kc_stored"], 16)
            pool.wait_ge(S["kc_stored"], 32)
            for t in range(2):
                pool.wait_ge(S[f"zT_stored{t}"], 160)
            kvT_h = kvT_d.rearrange("m (e d) t -> (m e) d t", e=2)
            qT_h = qT_d.rearrange("m (e d) t -> (m e) d t", e=2)

            def sample_loads(b, first=False):
                def ld(dst, src):
                    pool.dma_start(dst, src).then_inc(S["smp_loaded"], 16)

                if not first:
                    pool.wait_ge(S["so_ready"], b)
                new = bass.ds(SEQ + NT * b, NT)
                for g in range(PAGES):
                    page = pool.value_load(pt[0:1, bass.ds(PAGES * b + g, 1)], min_val=0, max_val=cache_sel.shape[1] - 1)
                    ld(kvp[:, 0, g, :], cache_sel[0][bass.ds(page, 1)].rearrange("g s c h e -> s (g c h e)"))
                ld(kvp[:, 1], cache_win[0][bass.ds(b, 1)].rearrange("b (g s) c h e -> s (b g) (c h e)", s=P))
                ld(vnew[:], kv_d[new, KVC:].rearrange("t (r c n) -> t r c n", r=2, c=2)[:, :, 1, :])
                for r in range(2):
                    ld(KTs[:, r, :, PAST:], kvT_d[4 * (r + 1):4 * (r + 1) + 2, :, new].rearrange("c p t -> p c t"))
                for e in range(2):
                    for c in range(2):
                        h = 2 * c + e
                        ld(qz[64 * e:64 * e + 64, h], qT_h[4 * h:4 * h + 4, :, new].rearrange("g d t -> d g t"))
                    ld(kc4[64 * e:64 * e + 64], kc_d.rearrange("(c e) d b -> e d c b", e=2)[e][:, :, bass.ds(8 + 4 * b, 4)])
                ld(vc4[:], vc_d[:, bass.ds(8 + 4 * b, 4), :].rearrange("h b e -> b h e"))

            def head_loads(i, first=False):
                def ld(dst, src):
                    pool.dma_start(dst, src).then_inc(S["head_loaded"], 16)

                if not first:
                    pool.wait_ge(S["pv_done"], 16 * i)
                h = i // 2
                for r in range(2):
                    ld(KTp[:, r, :], kvT_h[bass.ds(8 * (r + 1) + h, 1), :, 0:SEQ].rearrange("m d t -> d (m t)"))
                    ld(Vp[:, r], kv_d[0:SEQ, bass.ds(KVC * (r + 1) + 4 * HD + HD * h, HD)]
                       .rearrange("(t p) e -> p t e", p=P))
                    ld(qh[:, r, :], qT_h[bass.ds(2 * i + r, 1), :, 0:SEQ].rearrange("m d t -> d (m t)"))
                ld(kch[:], kc_d[bass.ds(h, 1), :, 0:8].rearrange("h d b -> d (h b)"))
                ld(vch[:], vc_d[bass.ds(h, 1), 0:8, :].rearrange("h b e -> (h b) e"))

            seq(pool.memset(qz[:], 0.0))
            sample_loads(0, first=True)
            head_loads(0, first=True)
            with pool.Fori(1, NB) as i:
                sample_loads(i)
                head_loads(i)

            for s in range(2):
                pool.wait_ge(S[f"zT_stored{s}"], 160 + 16 * 16)

            def mg_loads(i, first=False):
                for s in range(2):
                    if not first:
                        pool.wait_ge(S["merged"], 2 * i + s - 1)
                    for j in range(2):
                        pool.dma_start(mgl[s][:, j, :], mg_d[bass.ds(16 * j + 2 * i + s, 1)].rearrange("m p n -> p (m n)"))\
                            .then_inc(S[f"mg_loaded{s}"], 16)

            mg_loads(0, first=True)
            with pool.Fori(1, 8) as i:
                mg_loads(i)

            def x_loads(i, first=False):
                for s in range(2):
                    if first:
                        pool.wait_ge(S["merged"], 16)
                    else:
                        pool.wait_ge(S["acc_ready"], A_WO + 2 * i + s - 1)
                    col = bass.ds(P * (2 * i + s), P)
                    pool.dma_start(xr[s][:, 0:4, :], x_prompt[0].rearrange("(t p) n -> p t n", p=P)[:, :, col])\
                        .then_inc(S[f"xr_loaded{s}"], 16)
                    pool.dma_start(xr[s][0:NS, 4, :], x_sample.rearrange("b t n -> (b t) n")[:, col])\
                        .then_inc(S[f"xr_loaded{s}"], 16)

            x_loads(0, first=True)
            with pool.Fori(1, 8) as i:
                x_loads(i)

        @block.scalar
        def _(act):
            def hi(pair, slot, before=None):
                act.wait_ge(raw_full[slot], 16 * pair + 16)
                if before is not None:
                    act.wait_ge(S["acc_ready"], before)
                act.activation(w_hi[slot][:], raw[slot][:], ACT.Copy).then_inc(S["split_hi"], 1)

            act.wait_ge(S["small_loaded"], 80)
            act.wait_ge(S["stats_set"], 1)
            for t in range(TT):
                rows = P if t < 4 else NS
                act.wait_ge(S[f"x_loaded{t}"], 16)
                if t:
                    act.wait_ge(S["sq_done"], t)
                act.activation(junk[0:rows], xn[0:rows, t, :], ACT.Square, accum_out=st5[0][0:rows, t:t + 1])\
                    .then_inc(S["sq_done"], 1)
                if t == 1:
                    hi(0, 0)
            act.wait_ge(S["rstd_step"], 1)
            act.activation(st5[2][:, 0:TT], st5[1][:, 0:TT], ACT.Sqrt).then_inc(S["chain_a"], 1)
            for k in range(KT):
                act.wait_ge(S["acc_ready"], A_X + k + 1)
                act.activation(A_hi[:, k, :], flat(k % 2)[:, 0:TOK], ACT.Copy, scale=gmix[:, k:k + 1])\
                    .then_inc(S["x_hi"], 1)
            with act.Fori(0, 4) as i:
                for s in range(2):
                    hi(C_U // 2 + i + s, 1 - s, A_U + 2 * i + s)
            with act.Fori(0, 6) as i:
                for s in range(2):
                    hi(C_KV // 2 + i + s, 1 - s, A_KV + 2 * i + s)
            hi(C_PM // 2, 1, A_PM)
            act.wait_ge(S["ng_ready"], 1)
            act.wait_ge(S["zT_stored0"], 96)
            act.activation(halves(zT[0][:])[0:3 * HEADS], acc(3)[0:3 * HEADS], ACT.Exp, scale=-1.0)\
                .then_inc(S["gate_exp"], 1)
            act.wait_ge(S["pooled"], 8)
            act.activation(D_hi[:], dT[:], ACT.Copy).then_inc(S["d_high"], 1)
            hi(C_Q // 2, 0)

            def q_pair(i):
                for s in range(2):
                    j = 2 * i + s
                    if j == 7:
                        act.wait_ge(S["half_full0"], 16)
                    hi(C_Q // 2 + i + s, 1 - s, A_Q + j)

            def hidden(kv):
                act.wait_ge(S["w1_used"], 4 * kv + 4)
                if kv:
                    act.wait_ge(S["c2_ready"], 1)
                act.activation(peb[:], PS[:, 4, 80:81], ACT.Copy).then_inc(S["pe_out"], 1)
                act.wait_ge(S["pe_out"], kv + 1)
                for half in range(2):
                    act.activation(G[:, :, :, half].rearrange("p h t -> p t h"),
                                   PS[:, 4 + half, 0:80].rearrange("p (t h) -> p t h", h=NKV),
                                   ACT.Gelu_apprx_tanh, bias=peb[:]).then_inc(S["gelu_done"], 1)

            q_pair(0)
            q_pair(1)
            hidden(0)
            q_pair(2)
            q_pair(3)
            act.wait_ge(S["half_full1"], 16)
            hi(C_MG // 2, 1, A_MG)
            hidden(1)
            act.wait_ge(S["ng_turned"], 1)

            def gate_step(i, m):
                s, pair = m % 2, 2 * i + m // 2 + 1
                act.wait_ge(S["acc_ready"], A_MG + 4 * i + m + 1)
                act.wait_ge(S[f"zT_stored{s}"], 160 + 16 * (2 * i + m // 2))
                act.activation(halves(zT[s][:]), acc(s), ACT.Exp, scale=-1.0).then_inc(S["mg_exp"], 1)
                act.wait_ge(S[f"half_full{s}"], 16 * pair + 16)
                hi(C_MG // 2 + pair, s)

            def sample(b):
                act.wait_ge(S["smax_done"], b + 1)
                act.activation(pc4[:], PS[:, 6, 0:4], ACT.Exp, bias=nms[:, 0:1], accum_out=rss[:, 0:1])\
                    .then_inc(S["sexp_done"], 1)
                for r in range(2):
                    act.activation(Ps[:, r, :], PS[:, 4 + r, 0:KEYS], ACT.Exp, bias=nms[:, r + 1:r + 2],
                                   accum_out=rss[:, r + 1:r + 2]).then_inc(S["sexp_done"], 1)
                for r in range(2):
                    act.wait_ge(S["sPT_ready"], 2 * b + r + 1)
                    if r == 0:
                        act.activation(pcT4[:], PS[0:4, 6, 384:512], ACT.Copy)
                    act.activation(PTb[r][0:NT, 256:384], PS[0:NT, 6, 256:384], ACT.Copy)
                    act.activation(PTb[r][:, 0:256], PS[:, 6, 0:256], ACT.Copy).then_inc(S["sPT_copied"], 1)

            def head(i, par):
                def exps(t):
                    act.wait_ge(S["max_done"], 8 * i + 4 * par + t + 1)
                    for r in range(2):
                        act.activation(Pb[t % 2][:, r, 0:P * (t + 1)], PS[:, 4 + r, 0:P * (t + 1)], ACT.Exp,
                                       bias=nmx[:, t % 2, r:r + 1], accum_out=rsx[:, t % 2, r:r + 1])\
                            .then_inc(S["exp_done"], 1)

                def turned(k):
                    act.wait_ge(S["PT_ready"], 16 * i + 8 * par + k + 1)
                    n = P * (k // 2 + 1)
                    act.activation(PTb[k % 2][:, 0:n], PS[:, 6, 0:n], ACT.Copy).then_inc(S["PT_copied"], 1)

                act.wait_ge(S["cmask_done"], 2 * i + par + 1)
                act.activation(pcm[:], pcs[:], ACT.Exp).then_inc(S["cexp_done"], 1)
                exps(0)
                act.wait_ge(S["cPT_ready"], 2 * i + par + 1)
                act.activation(pcT[:], PS[0:8, 6, :], ACT.Copy).then_inc(S["cPT_copied"], 1)
                exps(1)
                turned(0)
                turned(1)
                exps(2)
                if par:
                    gate_step(i, 2)
                turned(2)
                turned(3)
                exps(3)
                turned(4)
                if not par:
                    gate_step(i, 1)
                for k in range(5, 8):
                    turned(k)
                if par:
                    gate_step(i, 3)

            with act.Fori(0, NB) as i:
                sample(i)
                gate_step(i, 0)
                head(i, 0)
                head(i, 1)

            act.wait_ge(S["acc_ready"], A_BR)
            act.wait_ge(S["bank7_free"], 2 * NB + 1)
            for k in range(KT):
                act.activation(A_hi[:, k, :], (oN if k < 8 else oP)[:, k % 8, :], ACT.Copy).then_inc(S["A_high"], 1)

            def br_pair(i, first=False, last=False):
                for s in range(2):
                    if not (first and s == 0):
                        if not (last and s == 1):
                            act.wait_ge(S[f"half_full{1 - s}"], 16 * (16 + i + s) + 16)
                        hi(C_BR // 2 + i + s, 1 - s, A_BR + 2 * i + s)
                    act.wait_ge(S["br_sum"], 2 * i + s + 1)
                    act.activation(B_hi[:, bass.ds(2 * i + s, 1), :], mgl[s][:, 0:1, :], ACT.Copy)\
                        .then_inc(S["br_high"], 1)

            br_pair(0, first=True)
            with act.Fori(1, 7) as i:
                br_pair(i)
            br_pair(7, last=True)
            with act.Fori(0, 8) as i:
                for s in range(2):
                    hi(C_WO // 2 + i + s, 1 - s, A_WO + 2 * i + s)

            def squares(done, base):
                for k in range(KT):
                    act.wait_ge(S["acc_free"], done)
                    if k >= 2 or base:
                        act.wait_ge(S["sq_used"], base + k - 1)
                    act.activation(sq[k % 2][:], x2T[:, k, :], ACT.Square).then_inc(S["sq_ready"], 1)

            squares(A_FF, 0)
            act.wait_ge(S["root_in"], 1)
            act.activation(rB[:], tB[:], ACT.Sqrt).then_inc(S["root_done"], 1)
            for k in range(KT):
                act.wait_ge(S["h_in"], k + 1)
                act.activation(B_hi[:, k, :], ff[k % 2][:], ACT.Copy, scale=gmlp[:, k:k + 1]).then_inc(S["h_high"], 1)

            def group(g, last=False):
                c0, a0 = C_FF // 2 + C_GROUP // 2 * g, A_FF + A_GROUP * g
                with act.Fori(0, UP_PAIRS) as i:
                    for s in range(2):
                        hi(c0 + i + s, 1 - s, a0 + 2 * i + s)
                        act.wait_ge(S["acc_ready"], a0 + 2 * i + s + 1)
                        act.wait_ge(S["acc_free"], a0 + 2 * i + s - 1)
                        act.activation(halves(ff[s][:]), acc(s), ACT.Relu).then_inc(S["ff_relu"], 1)
                        act.wait_ge(S["ff_relu"], GK * g + 2 * i + s + 1)
                        act.activation(F_hi[:, bass.ds(2 * i + s, 1), :].rearrange("p k n -> p (k n)"), ff[s][:],
                                       ACT.Square).then_inc(S["ff_high"], 1)

                def down(i, last):
                    for s in range(2):
                        if not (last and s == 1):
                            hi(c0 + UP_PAIRS + i + s, 1 - s, a0 + GK + 4 * i + 2 * s)

                with act.Fori(0, DOWN_PAIRS - 1) as i:
                    down(i, False)
                down(DOWN_PAIRS - 1, last)

            with act.Fori(0, FFG - 1) as g:
                group(g)
            group(FFG - 1, last=True)
            squares(A_FF + A_GROUP * FFG, KT)
            act.wait_ge(S["root_in"], 2)
            act.activation(rF[:], tF[:], ACT.Sqrt).then_inc(S["root_done"], 1)
            with act.Fori(0, 8) as i:
                for s in range(2):
                    act.wait_ge(S["yT_in"], 2 * i + s + 1)
                    act.activation(yT[s][:], yT[s][:], ACT.Copy, scale=gfin[:, bass.ds(2 * i + s, 1)])\
                        .then_inc(S["yT_scaled"], 1)

        @block.vector
        def _(dve):
            n = [0]

            def seq(ins):
                n[0] += 1
                ins.then_inc(S["chain_v"], 1)
                dve.wait_ge(S["chain_v"], n[0])

            def lo(n, slot):
                dve.wait_ge(S["split_hi"], n + 1)
                dve.tensor_tensor(w_lo[slot][:], raw[slot][:], w_hi[slot][:].bitcast(F32), ALU.subtract)\
                    .then_inc(S["split_lo"], 1)

            ss, v, r, q = (st5[j][:, 0:TT] for j in range(4))
            lo(0, 0)
            dve.wait_ge(S["sq_done"], TT)
            dve.tensor_scalar(v, ss, 1.0 / D, EPS, ALU.mult, ALU.add).then_inc(S["rstd_step"], 1)
            dve.wait_ge(S["chain_a"], 1)
            seq(dve.reciprocal(r, r))
            seq(dve.tensor_tensor(q, r, r, ALU.mult))
            seq(dve.tensor_tensor(q, q, v, ALU.mult))
            seq(dve.tensor_scalar(q, q, -0.5, 1.5, ALU.mult, ALU.add))
            seq(dve.tensor_tensor(r, r, q, ALU.mult))
            for t in range(TT):
                rows = P if t < 4 else NS
                dve.tensor_scalar(xn[0:rows, t, :], xn[0:rows, t, :], r[0:rows, t:t + 1], None, ALU.mult)\
                    .then_inc(S["x_scaled"], 1)
            dve.wait_ge(S["consts_ready"], 1)
            dve.reciprocal(rc[:], rc[:]).then_inc(S["rc_done"], 1)
            dve.wait_ge(S["st_ready"], 1)
            dve.tensor_copy(stT[:].rearrange("p (h m) r -> p h (m r)", h=2), PS[:, 4:6, 0:4 * NB * PSTATE])\
                .then_inc(S["st_copied"], 1)
            for k in range(KT):
                dve.wait_ge(S["x_hi"], k + 1)
                dve.scalar_tensor_tensor(out=A_lo[:, k, :], in0=flat(k % 2)[:, 0:TOK], scalar=gmix[:, k:k + 1],
                                         in1=A_hi[:, k, :].bitcast(F32), op0=ALU.mult, op1=ALU.subtract)\
                    .then_inc(S["acc_free"], 1)
            with dve.Fori(0, 4) as i:
                for s in range(2):
                    lo(C_U + 2 * i + s + 1, 1 - s)
                    dve.wait_ge(S["acc_ready"], A_U + 2 * i + s + 1)
                    dve.tensor_copy(uT[:, bass.ds(2 * i + s, 1), :].rearrange("p m (h n) -> p (m h) n", h=2), acc(s))\
                        .then_inc(S["acc_free"], 1)
            dve.wait_ge(S["tail_ready"], 1)
            for j in range(2):
                dve.tensor_copy(unat[:, 512 * j:512 * j + 512], PS[0:79, 4 + 2 * j, :]).then_inc(S[f"zn_done{j}"], 1)

            def kv_pair(i, first=False):
                for s in range(2):
                    lo(C_KV + 2 * i + s + 1, 1 - s)
                    dve.wait_ge(S["acc_ready"], A_KV + 2 * i + s + 1)
                    if not first:
                        dve.wait_ge(S[f"zT_stored{s}"], 16 * i)
                    dve.tensor_copy(halves(zT[s][:]), acc(s)).then_inc(S["acc_free"], 1)
                for s in range(2):
                    dve.wait_ge(S[f"nat_ready{s}"], i + 1)
                    if not first:
                        dve.wait_ge(S[f"zn_stored{s}"], 32 * i)
                    dve.tensor_copy(zn[s][:, 0:4, :].rearrange("p t n -> p (t n)"), flat(2 + s)[:, 0:SEQ])\
                        .then_inc(S[f"zn_done{s}"], 1)
                    dve.tensor_copy(zn[s][0:NS, 4, :], flat(2 + s)[0:NS, SEQ:]).then_inc(S[f"zn_done{s}"], 1)

            kv_pair(0, first=True)
            with dve.Fori(1, 6) as i:
                kv_pair(i)
            lo(C_NG + 1, 1)
            gT = zT[0][0:3 * HEADS]
            dve.wait_ge(S["gate_exp"], 1)
            seq(dve.tensor_scalar(gT, gT, 1.0, None, ALU.add))
            dve.reciprocal(gT, gT).then_inc(S["gateT_done"], 1)
            dve.wait_ge(S["tail_stored"], 32)
            dve.wait_ge(S["d_high"], 1)
            dve.tensor_tensor(D_lo[:], dT[:], D_hi[:].bitcast(F32), ALU.subtract).then_inc(S["d_ready"], 1)
            lo(C_PM + 1, 0)
            for m in range(8):
                dve.wait_ge(S["acc_ready"], A_PM + m + 1)
                dve.tensor_scalar(halves(oP[:, m, :]), acc(m % 2), psc[:, m:m + 1], None, ALU.mult)\
                    .then_inc(S["acc_free"], 1)
            dve.wait_ge(S["ng_turned"], 1)
            dve.tensor_copy(gn[:], PS[0:NS, 6, 192:240]).then_inc(S["bank7_free"], 1)
            seq(dve.tensor_copy(gp[:].rearrange("p t n -> p (t n)"), PS[:, 6, 0:192]))
            dve.tensor_scalar(gp[:, 0, 0:HEADS], gp[:, 0, 0:HEADS], vis[:, 0:1], None, ALU.mult)\
                .then_inc(S["gates_done"], 1)
            def q_pair(i):
                for s in range(2):
                    lo(C_Q + 2 * i + s + 1, 1 - s)
                    dve.wait_ge(S["acc_ready"], A_Q + 2 * i + s + 1)
                    dve.wait_ge(S[f"zT_stored{s}"], 16 * (6 + i))
                    dve.tensor_scalar(halves(zT[s][:]), acc(s), HD ** -0.5, None, ALU.mult).then_inc(S["acc_free"], 1)

            for i in range(3):
                q_pair(i)
            dve.wait_ge(S["c2_ready"], 1)
            dve.tensor_copy(kcs[:].rearrange("e h b -> e (h b)"), PS[0:HD, 6, 0:160]).then_inc(S["c2_done"], 1)
            q_pair(3)
            lo(C_MG + 1, 1)
            dve.wait_ge(S["c2_ready"], 2)
            dve.tensor_copy(vcs[:].rearrange("b h e -> b (h e)"), PS[0:40, 6, 0:256]).then_inc(S["c2_done"], 1)
            dve.wait_ge(S["gs_loaded"], 16 * 48)

            def gate_step(i, m):
                s, a = m % 2, A_MG + 4 * i + m + 1
                dve.wait_ge(S["mg_exp"], 4 * i + m + 1)
                dve.tensor_scalar(zT[s][:], zT[s][:], 1.0, None, ALU.add).then_inc(S["acc_free"], 1)
                dve.wait_ge(S["acc_free"], a)
                dve.reciprocal(zT[s][:], zT[s][:]).then_inc(S["mg_done"], 1)
                lo(C_MG + 4 * i + m + 2, s)

            local = [0]

            def linked(i, ins):
                local[0] += 1
                ins.then_inc(S["chain_att"], 1)
                dve.wait_ge(S["chain_att"], (CHAIN_SMP + 2 * CHAIN_HEAD) * i + local[0])

            def sample(b):
                dve.wait_ge(S["KT_ready"], b + 1)
                dve.tensor_copy(KTs[:, :, :, 0:PAST], PS[:, 4:6, :].rearrange("p r (c n) -> p r c n", c=2))\
                    .then_inc(S["KT_copied"], 1)
                dve.wait_ge(S["ss_ready"], b + 1)
                dve.tensor_reduce(nms[:, 0:1], PS[:, 6, 0:4], X, ALU.max, negate=True)
                linked(b, dve.tensor_tensor(PS[:, 4:6, PAST:KEYS], PS[:, 4:6, PAST:KEYS],
                                            smask[:].unsqueeze(1).broadcast_to([P, 2, NT]), ALU.add))
                dve.tensor_reduce(nms[:, 1:3], PS[:, 4:6, 0:KEYS], X, ALU.max, negate=True).then_inc(S["smax_done"], 1)
                dve.wait_ge(S["sexp_done"], 3 * b + 3)
                linked(b, dve.reciprocal(wsm[:, 0:3], rss[:, 0:3]))
                linked(b, dve.tensor_tensor(wsm[:, 0:3].unsqueeze(1), wsm[:, 0:3].unsqueeze(1), gs[:, bass.ds(b, 1), :],
                                            ALU.mult))
                dve.tensor_scalar(pc4[:], pc4[:], wsm[:, 0:1], None, ALU.mult)
                for r in range(2):
                    dve.tensor_scalar(Ps[:, r, :], Ps[:, r, :], wsm[:, r + 1:r + 2], None, ALU.mult)\
                        .then_inc(S["sP_ready"], 1)
                gate_step(b, 0)
                dve.wait_ge(S["so_ready"], b + 1)
                dve.tensor_copy(oN[:, :, bass.ds(SEQ + NT * b, NT)], PS[:, 7, 0:64].rearrange("p (k t) -> p k t", t=NT))\
                    .then_inc(S["bank7_free"], 1)

            def head(i, par):
                def top(t):
                    dve.wait_ge(S["s_ready"], 8 * i + 4 * par + t + 1)
                    dve.tensor_reduce(nmx[:, t % 2, :], PS[:, 4:6, 0:P * (t + 1)], X, ALU.max, negate=True)\
                        .then_inc(S["max_done"], 1)

                def weigh(t):
                    dve.wait_ge(S["exp_done"], 16 * i + 8 * par + 2 * t + 2)
                    linked(i, dve.reciprocal(wx[:, t % 2, :], rsx[:, t % 2, :]))
                    g = gp[:, t, HEADS:].rearrange("p (r n) -> p r n", r=2)[:, :, bass.ds(2 * i + par, 1)]
                    linked(i, dve.tensor_tensor(wx[:, t % 2, :].unsqueeze(2), wx[:, t % 2, :].unsqueeze(2), g, ALU.mult))
                    for r in range(2):
                        part = Pb[t % 2][:, r, 0:P * (t + 1)]
                        dve.tensor_scalar(part, part, wx[:, t % 2, r:r + 1], None, ALU.mult).then_inc(S["P_ready"], 1)

                dve.wait_ge(S["cs_ready"], 2 * i + par + 1)
                linked(i, dve.tensor_tensor(pcs[:], PS[:, 6, 0:32].rearrange("p (t b) -> p t b", b=8), bmask[:], ALU.add))
                linked(i, dve.tensor_reduce(nmc[:], pcs[:], X, ALU.max))
                dve.tensor_tensor(pcs[:], pcs[:], nmc[:].unsqueeze(2).broadcast_to([P, 4, 8]), ALU.subtract)\
                    .then_inc(S["cmask_done"], 1)
                top(0)
                dve.wait_ge(S["cexp_done"], 2 * i + par + 1)
                linked(i, dve.tensor_reduce(rsc[:], pcm[:], X, ALU.add))
                linked(i, dve.reciprocal(wc[:], rsc[:]))
                linked(i, dve.tensor_tensor(wc[:].unsqueeze(2), wc[:].unsqueeze(2), gp[:, :, bass.ds(2 * i + par, 1)],
                                            ALU.mult))
                dve.tensor_tensor(pcm[:], pcm[:], wc[:].unsqueeze(2).broadcast_to([P, 4, 8]), ALU.mult)\
                    .then_inc(S["cP_ready"], 1)
                weigh(0)
                for t in range(1, 4):
                    top(t)
                    weigh(t)
                    if par and t == 2:
                        gate_step(i, 2)
                gate_step(i, 3 if par else 1)

            with dve.Fori(0, NB) as i:
                sample(i)
                head(i, 0)
                head(i, 1)
                dve.wait_ge(S["pv_done"], 16 * i + 16)
                dve.tensor_copy(oN[:, bass.ds(i, 1), 0:SEQ], PS[:, 7:8, :]).then_inc(S["bank7_free"], 1)
            assert local[0] == CHAIN_SMP + 2 * CHAIN_HEAD

            for k in range(KT):
                dve.wait_ge(S["A_high"], k + 1)
                dve.tensor_tensor(A_lo[:, k, :], (oN if k < 8 else oP)[:, k % 8, :], A_hi[:, k, :].bitcast(F32),
                                  ALU.subtract).then_inc(S["A_split"], 1)
            def br_pair(i, first=False):
                for s in range(2):
                    j = 2 * i + s
                    if not (first and s == 0):
                        lo(C_BR + j + 1, 1 - s)
                    dve.wait_ge(S["acc_ready"], A_BR + j + 1)
                    dve.wait_ge(S[f"mg_loaded{s}"], 32 * i + 32)
                    pair = acc(s, 4)
                    dve.tensor_tensor(halves(mgl[s][:, 0, :]), pair[:, 0:2, :], halves(mgl[s][:, 0, :]), ALU.mult)
                    dve.tensor_tensor(halves(mgl[s][:, 1, :]), pair[:, 2:4, :], halves(mgl[s][:, 1, :]), ALU.mult)\
                        .then_inc(S["acc_free"], 1)
                    dve.wait_ge(S["acc_free"], A_BR + j + 1)
                    dve.tensor_tensor(mgl[s][:, 0, :], mgl[s][:, 0, :], mgl[s][:, 1, :], ALU.add).then_inc(S["br_sum"], 1)
                    dve.wait_ge(S["br_high"], j + 1)
                    dve.tensor_tensor(B_lo[:, bass.ds(j, 1), :], mgl[s][:, 0:1, :],
                                      B_hi[:, bass.ds(j, 1), :].bitcast(F32), ALU.subtract).then_inc(S["merged"], 1)

            br_pair(0, first=True)
            with dve.Fori(1, 8) as i:
                br_pair(i)
            with dve.Fori(0, 8) as i:
                for s in range(2):
                    j = 2 * i + s
                    lo(C_WO + j + 1, 1 - s)
                    tile_ = x2T[:, bass.ds(j, 1), :].rearrange("p m (h n) -> p (m h) n", h=2)
                    dve.wait_ge(S["x_turned"], j + 1)
                    dve.tensor_copy(tile_, acc(2 + s)).then_inc(S["xT_copied"], 1)
                    dve.wait_ge(S["xT_copied"], j + 1)
                    dve.wait_ge(S["acc_ready"], A_WO + j + 1)
                    dve.tensor_tensor(tile_, acc(s), tile_, ALU.add)\
                        .then_inc(S["acc_free"], 1)

            def inverse_root(k, r, v, t):
                dve.wait_ge(S["sq_used"], KT * k + KT)
                dve.tensor_scalar(halves(v[:]), acc(2), 1.0 / D, EPS, ALU.mult, ALU.add).then_inc(S["root_in"], 1)
                dve.wait_ge(S["root_done"], k + 1)
                seq(dve.reciprocal(r[:], r[:]))
                seq(dve.tensor_tensor(t[:], r[:], r[:], ALU.mult))
                seq(dve.tensor_tensor(t[:], t[:], v[:], ALU.mult))
                seq(dve.tensor_scalar(t[:], t[:], -0.5, 1.5, ALU.mult, ALU.add))
                seq(dve.tensor_tensor(r[:], r[:], t[:], ALU.mult))

            inverse_root(0, rB, tB, ff[0])
            for k in range(KT + 1):
                if k < KT:
                    if k >= 2:
                        dve.wait_ge(S["h_ready"], k - 1)
                    dve.tensor_tensor(ff[k % 2][:], x2T[:, k, :], rB[:], ALU.mult).then_inc(S["h_in"], 1)
                if k:
                    j = k - 1
                    dve.wait_ge(S["h_high"], j + 1)
                    dve.scalar_tensor_tensor(out=B_lo[:, j, :], in0=ff[j % 2][:], scalar=gmlp[:, j:j + 1],
                                             in1=B_hi[:, j, :].bitcast(F32), op0=ALU.mult, op1=ALU.subtract)\
                        .then_inc(S["h_ready"], 1)

            def group(g, last=False):
                c0, a0 = C_FF + C_GROUP * g, A_FF + A_GROUP * g
                with dve.Fori(0, UP_PAIRS) as i:
                    for s in range(2):
                        j = 2 * i + s
                        lo(c0 + j + 1, 1 - s)
                        dve.wait_ge(S["ff_relu"], GK * g + j + 1)
                        dve.tensor_tensor(ff2[s][:], ff[s][:], ff[s][:], ALU.mult).then_inc(S["acc_free"], 1)
                        dve.wait_ge(S["acc_free"], a0 + j + 1)
                        dve.wait_ge(S["ff_high"], GK * g + j + 1)
                        dve.tensor_tensor(F_lo[:, bass.ds(j, 1), :].rearrange("p k n -> p (k n)"), ff2[s][:],
                                          F_hi[:, bass.ds(j, 1), :].rearrange("p k n -> p (k n)").bitcast(F32),
                                          ALU.subtract).then_inc(S["ff_ready"], 1)

                def down(i, last):
                    for s in range(2):
                        if not (last and s == 1):
                            lo(c0 + GK + 2 * i + s + 1, 1 - s)
                        for e in range(2):
                            m = 4 * i + 2 * s + e
                            dve.wait_ge(S["acc_ready"], a0 + GK + m + 1)
                            tile_ = x2T[:, bass.ds(m, 1), :].rearrange("p m (h n) -> p (m h) n", h=2)
                            dve.tensor_tensor(tile_, acc(e), tile_, ALU.add).then_inc(S["acc_free"], 1)

                with dve.Fori(0, DOWN_PAIRS - 1) as i:
                    down(i, False)
                down(DOWN_PAIRS - 1, last)

            with dve.Fori(0, FFG - 1) as g:
                group(g)
            group(FFG - 1, last=True)
            inverse_root(1, rF, tF, yT[0])

            def y_pair(i, first=False):
                for s in range(2):
                    dve.tensor_tensor(yT[s][:].unsqueeze(1), x2T[:, bass.ds(2 * i + s, 1), :], rF[:].unsqueeze(1), ALU.mult)\
                        .then_inc(S["yT_in"], 1)
                for s in range(2):
                    dve.wait_ge(S["y_turned"], 2 * i + s + 1)
                    if not first:
                        dve.wait_ge(S[f"yn_stored{s}"], 32 * i)
                    dve.tensor_copy(yn[s][:, 0:4, :].rearrange("p t n -> p (t n)"), flat(s)[:, 0:SEQ])\
                        .then_inc(S["yn_done"], 1)
                    dve.tensor_copy(yn[s][0:NS, 4, :], flat(s)[0:NS, SEQ:]).then_inc(S["yn_done"], 1)

            y_pair(0, first=True)
            with dve.Fori(1, 8) as i:
                y_pair(i)

        @block.tensor
        def _(pe):
            def product(w_slot, mhi, mlo, dst, ks, wk=0, first=True, last=True, width=P, col=0, ready=None):
                for j, k in enumerate(ks):
                    cut = slice((wk + j) * width + col, (wk + j) * width + col + P)
                    if ready is not None:
                        pe.wait_ge(S[ready], k + 1)
                    wh, wl = w_hi[w_slot][:, cut], w_lo[w_slot][:, cut]
                    for a, (w, x) in enumerate(((wh, mhi), (wh, mlo), (wl, mhi))):
                        for h in range(2):
                            ins = pe.matmul(dst[:, h, :], w, x[:, k, HALF * h:HALF * h + HALF],
                                            start=first and j == 0 and a == 0,
                                            stop=last and j == len(ks) - 1 and a == 2)
                return ins

            def tile(n, a, s):
                pe.wait_ge(S["split_lo"], n + 1)
                pe.wait_ge(S["acc_free"], a - 1)
                product(s, A_hi, A_lo, acc(s), range(KT)).then_inc(S["acc_ready"], 1)

            pe.wait_ge(S["consts_ready"], 1)
            pe.wait_ge(S["state_loaded"], 16)
            for m in range(8):
                ins = pe.transpose(PS[:, 4 + m // 4, 120 * (m % 4):120 * (m % 4) + 120], stN[:, m * P:(m + 1) * P],
                                   ident[0:120, 0:120])
            ins.then_inc(S["st_ready"], 1)
            pe.wait_ge(S["x_scaled"], TT)
            for k in range(KT):
                if k >= 2:
                    pe.wait_ge(S["acc_free"], k - 1)
                for t in range(TT):
                    rows = P if t < 4 else NS
                    ins = pe.transpose(flat(k % 2)[:, t * P:t * P + rows], xn[0:rows, t, k * P:(k + 1) * P],
                                       ident[0:rows, 0:rows])
                ins.then_inc(S["acc_ready"], 1)
            pe.wait_ge(S["acc_free"], KT)
            with pe.Fori(0, 4) as i:
                for s in range(2):
                    tile(C_U + 2 * i + s, A_U + 2 * i + s, s)
            pe.wait_ge(S["acc_free"], A_KV)
            pe.wait_ge(S["st_copied"], 1)
            for m in range(8):
                ins = pe.transpose(PS[0:79, 4 + 2 * (m // 4), P * (m % 4):P * (m % 4) + P], uT[:, m, SEQ - PSTATE:TOK], ident[:])
            ins.then_inc(S["tail_ready"], 1)
            with pe.Fori(0, 6) as i:
                for s in range(2):
                    tile(C_KV + 2 * i + s, A_KV + 2 * i + s, s)
                for s in range(2):
                    pe.wait_ge(S["acc_free"], A_KV + 2 * i + s + 1)
                    pe.wait_ge(S[f"zn_done{s}"], 2 * i + 1)
                    for t in range(TT):
                        rows = P if t < 4 else NS
                        ins = pe.transpose(flat(2 + s)[0:rows, t * P:(t + 1) * P], zT[s][:, t * P:t * P + rows], ident[:])
                    ins.then_inc(S[f"nat_ready{s}"], 1)
            pe.wait_ge(S["split_lo"], C_NG + 1)
            for s in range(2):
                pe.wait_ge(S[f"zn_done{s}"], 13)
            product(0, A_hi, A_lo, acc(3), range(KT)).then_inc(S["ng_ready"], 1)
            pe.wait_ge(S["split_lo"], C_PM + 1)
            pe.wait_ge(S["d_ready"], 1)
            for m in range(8):
                g = m // 2
                pe.wait_ge(S["acc_free"], A_PM + m - 1)
                product(1, D_hi, D_lo, acc(m % 2), (2 * g, 2 * g + 1), wk=2 * g, width=256, col=P * (m % 2))\
                    .then_inc(S["acc_ready"], 1)
            pe.wait_ge(S["gateT_done"], 1)
            for t in range(TT):
                rows = P if t < 4 else NS
                ins = pe.transpose(PS[0:rows, 6, 48 * t:48 * t + 48], zT[0][0:48, t * P:t * P + rows], ident[0:48, 0:48])
            ins.then_inc(S["ng_turned"], 1)
            def hidden(kv):
                pe.wait_ge(S["crow_loaded"], 288 * kv + 288)
                if kv:
                    pe.wait_ge(S["gelu_done"], 2)
                rows = crow[:].rearrange("p t h e -> p (t h) e")
                for q in range(4):
                    c = 4 * kv + q
                    pe.wait_ge(S[f"w1_loaded{c % 2}"], 32 * (c // 2) + 32)
                    for d in range(16):
                        for half in range(2):
                            n = 81 if half == 0 else 80
                            ins = pe.matmul(PS[:, 4 + half, 0:n], w1[c % 2][64 * half:64 * half + 64, d, :],
                                            rows[64 * half:64 * half + 64, 0:n, 16 * q + d],
                                            start=q == 0 and d == 0, stop=q == 3 and d == 15)
                    ins.then_inc(S["w1_used"], 1)

            def q_pair(i):
                for s in range(2):
                    tile(C_Q + 2 * i + s, A_Q + 2 * i + s, s)

            q_pair(0)
            q_pair(1)
            hidden(0)
            q_pair(2)
            pe.wait_ge(S["w2_loaded"], 32)
            pe.wait_ge(S["gelu_done"], 2)
            pe.wait_ge(S["gates_done"], 1)
            pe.matmul(PS[0:HD, 6, 0:160], w2[0][:], G[:].rearrange("p h t g -> p (h t g)"), start=True, stop=True)\
                .then_inc(S["c2_ready"], 1)
            q_pair(3)
            hidden(1)
            pe.wait_ge(S["gelu_done"], 4)
            pe.wait_ge(S["c2_done"], 1)
            for h in range(NKV):
                ins = pe.matmul(PS[0:40, 6, HD * h:HD * h + HD], G[:, h].rearrange("p t g -> p (t g)"), w2[1][:],
                                start=True, stop=True)
            ins.then_inc(S["c2_ready"], 1)
            pe.wait_ge(S["c2_done"], 2)

            def gate_part(i, m, k0, n):
                s = m % 2
                if k0 == 0:
                    pe.wait_ge(S["split_lo"], C_MG + 4 * i + m + 1)
                    pe.wait_ge(S["acc_free"], A_MG + 4 * i + m - 1)
                ins = product(s, A_hi, A_lo, acc(s), range(k0, k0 + n), wk=k0, first=k0 == 0, last=k0 + n == KT)
                if k0 + n == KT:
                    ins.then_inc(S["acc_ready"], 1)

            def sample(b):
                pe.wait_ge(S["smp_loaded"], 16 * SMP_DMAS * b + 16 * SMP_DMAS)
                for r in range(2):
                    for c in range(2):
                        for g in range(PAGES):
                            ins = pe.transpose(PS[:, 4 + r, 256 * c + P * g:256 * c + P * g + P],
                                               kvp[:, r, g, P * c:P * c + P], ident[:])
                ins.then_inc(S["KT_ready"], 1)
                gate_part(b, 0, 0, 4)
                pe.wait_ge(S["KT_copied"], b + 1)
                for r in range(2):
                    for h in range(NKV):
                        c = h // 2
                        pe.matmul(PS[32 * h:32 * h + 32, 4 + r, 0:KEYS], qz[:, h].rearrange("p g t -> p (g t)"),
                                  KTs[:, r, c, :], start=True, stop=True)
                for h in range(NKV):
                    c = h // 2
                    ins = pe.matmul(PS[32 * h:32 * h + 32, 6, 0:4], qz[:, h].rearrange("p g t -> p (g t)"),
                                    kc4[:, c, :], start=True, stop=True)
                ins.then_inc(S["ss_ready"], 1)
                gate_part(b, 0, 4, 8)
                for r in range(2):
                    pe.wait_ge(S["sP_ready"], 2 * b + r + 1)
                    if r == 0:
                        pe.transpose(PS[0:4, 6, 384:512], pc4[:], ident[:])
                    else:
                        pe.wait_ge(S["sPT_copied"], 2 * b + 1)
                    pe.transpose(PS[0:NT, 6, 256:384], Ps[:, r, PAST:], ident[:])
                    for g in range(PAGES):
                        ins = pe.transpose(PS[:, 6, P * g:P * g + P], Ps[:, r, P * g:P * g + P], ident[:])
                    ins.then_inc(S["sPT_ready"], 1)
                gate_part(b, 0, 12, 4)
                pe.wait_ge(S["sPT_copied"], 2 * b + 2)
                pe.wait_ge(S["bank7_free"], 2 * b + 1)
                for h in range(NKV):
                    for e in range(2):
                        def mine(pT):
                            return pT[:, 32 * h:32 * h + 32].rearrange("p (k e t) -> p k e t", e=2, t=NT)[:, :, e, :]

                        out = PS[64 * e:64 * e + 64, 7, 16 * h:16 * h + 16].rearrange("p (k t) -> p k t", t=NT)
                        pe.matmul(out, vc4[:, h, :], mine(pcT4[:]), start=True, stop=False, skip_group_check=True)
                        for r in range(2):
                            for g in range(PAGES):
                                pe.matmul(out, kvp[:, r, g, 256 + HD * h:256 + HD * h + HD], mine(PTb[r][:, P * g:P * g + P]),
                                          start=False, stop=False, skip_group_check=True)
                            ins = pe.matmul(out, vnew[:, r, HD * h:HD * h + HD], mine(PTb[r][0:NT, 256:384]),
                                            start=False, stop=r == 1, skip_group_check=True)
                ins.then_inc(S["so_ready"], 1)

            def head(i, par):
                def scores(t):
                    if par == 0 and t == 0:
                        pe.wait_ge(S["sexp_done"], 3 * i + 3)
                    else:
                        pe.wait_ge(S["exp_done"], 16 * i + 8 * par + 2 * t)
                    n = P * (t + 1)
                    for r in range(2):
                        pe.matmul(PS[:, 4 + r, P * t:n], identb[:], cmask[:], start=True, stop=False)
                        ins = pe.matmul(PS[:, 4 + r, P * t:n], qh[:, par, P * t:n], KTp[:, r, P * t:n], start=False, stop=True)
                        if t:
                            ins = pe.matmul(PS[:, 4 + r, 0:P * t], qh[:, par, P * t:n], KTp[:, r, 0:P * t],
                                            start=True, stop=True)
                    ins.then_inc(S["s_ready"], 1)

                def turn(k):
                    t, r = k // 2, k % 2
                    pe.wait_ge(S["P_ready"], 16 * i + 8 * par + k + 1)
                    if k:
                        pe.wait_ge(S["PT_copied"], 16 * i + 8 * par + k)
                    else:
                        pe.wait_ge(S["cPT_copied"], 2 * i + par + 1)
                    for j in range(t + 1):
                        ins = pe.transpose(PS[:, 6, P * j:P * j + P], Pb[t % 2][:, r, P * j:P * j + P], ident[:])
                    ins.then_inc(S["PT_ready"], 1)

                def values(k):
                    t, r = k // 2, k % 2
                    pe.wait_ge(S["PT_copied"], 16 * i + 8 * par + k + 1)
                    for j in range(t + 1):
                        ins = pe.matmul(PS[64 * par:64 * par + 64, 7, P * t:P * t + P], Vp[:, r, j, :],
                                        PTb[k % 2][:, P * j:P * j + P], start=False, stop=k == 7 and j == t)
                    ins.then_inc(S["pv_done"], 1)

                def between(p):
                    u = 24 * par + 2 * p
                    gate_part(i, 1 + u // KT, u % KT, 2)

                if par:
                    pe.wait_ge(S["PT_copied"], 16 * i + 8)
                for t in range(4):
                    ins = pe.matmul(PS[:, 6, 8 * t:8 * t + 8], qh[:, par, P * t:P * t + P], kch[:], start=True, stop=True)
                ins.then_inc(S["cs_ready"], 1)
                scores(0)
                between(0)
                between(1)
                pe.wait_ge(S["cP_ready"], 2 * i + par + 1)
                for t in range(4):
                    ins = pe.transpose(PS[0:8, 6, P * t:P * t + P], pcm[:, t, :], ident[:])
                ins.then_inc(S["cPT_ready"], 1)
                scores(1)
                between(2)
                turn(0)
                pe.wait_ge(S["bank7_free"], 2 * i + 2)
                pe.matmul(PS[64 * par:64 * par + 64, 7, :], vch[:], pcT[:], start=True, stop=False)
                between(3)
                for k in range(8):
                    if k < 7:
                        turn(k + 1)
                    between(4 + k)
                    values(k)
                    if k in (0, 2):
                        scores(k // 2 + 2)

            with pe.Fori(0, NB) as i:
                sample(i)
                pe.wait_ge(S["head_loaded"], 16 * HEAD_DMAS * i + 16 * HEAD_DMAS)
                head(i, 0)
                head(i, 1)

            pe.wait_ge(S["acc_free"], A_BR)
            pe.wait_ge(S["bank7_free"], 2 * NB + 1)
            with pe.Fori(0, 8) as i:
                for s in range(2):
                    pe.wait_ge(S["split_lo"], C_BR + 2 * i + s + 1)
                    pe.wait_ge(S["acc_free"], A_BR + 2 * i + s - 1)
                    product(s, A_hi, A_lo, acc(s, 4)[:, 0:2, :], range(8), ready="A_split")
                    product(s, A_hi, A_lo, acc(s, 4)[:, 2:4, :], range(8, KT), wk=8, ready="A_split").then_inc(S["acc_ready"], 1)
            pe.wait_ge(S["merged"], KT)
            with pe.Fori(0, 8) as i:
                for s in range(2):
                    pe.wait_ge(S["split_lo"], C_WO + 2 * i + s + 1)
                    pe.wait_ge(S["acc_free"], A_WO + 2 * i + s - 1)
                    pe.wait_ge(S[f"xr_loaded{s}"], 32 * i + 32)
                    for t in range(TT):
                        rows = P if t < 4 else NS
                        for h in range(2):
                            a, b = max(P * t, HALF * h), min(P * t + rows, HALF * h + HALF)
                            if a < b:
                                ins = pe.matmul(acc(2 + s)[:, h, a - HALF * h:b - HALF * h], xr[s][0:rows, t, :],
                                                ident[0:rows, a - P * t:b - P * t], start=True, stop=True)
                    ins.then_inc(S["x_turned"], 1)
                    product(s, B_hi, B_lo, acc(s), range(KT)).then_inc(S["acc_ready"], 1)

            def square_sums(base):
                for k in range(KT):
                    pe.wait_ge(S["sq_ready"], base + k + 1)
                    for h in range(2):
                        ins = pe.matmul(acc(2)[:, h, :], onesm[:], halves(sq[k % 2][:])[:, h, :], start=k == 0,
                                        stop=k == KT - 1)
                    ins.then_inc(S["sq_used"], 1)

            pe.wait_ge(S["acc_free"], A_FF)
            square_sums(0)

            def group(g):
                c0, a0 = C_FF + C_GROUP * g, A_FF + A_GROUP * g
                with pe.Fori(0, UP_PAIRS) as i:
                    for s in range(2):
                        pe.wait_ge(S["split_lo"], c0 + 2 * i + s + 1)
                        pe.wait_ge(S["acc_free"], a0 + 2 * i + s - 1)
                        product(s, B_hi, B_lo, acc(s), range(KT), ready="h_ready").then_inc(S["acc_ready"], 1)
                with pe.Fori(0, DOWN_PAIRS) as i:
                    for s in range(2):
                        pe.wait_ge(S["split_lo"], c0 + GK + 2 * i + s + 1)
                        if s == 0:
                            pe.wait_ge(S["ff_ready"], GK * g + GK)
                        for e in range(2):
                            pe.wait_ge(S["acc_free"], a0 + GK + 4 * i + 2 * s + e - 1)
                            product(s, F_hi, F_lo, acc(e), range(GK), width=256, col=P * e).then_inc(S["acc_ready"], 1)

            with pe.Fori(0, FFG) as g:
                group(g)
            square_sums(KT)
            with pe.Fori(0, 8) as i:
                for s in range(2):
                    pe.wait_ge(S["yT_scaled"], 2 * i + s + 1)
                    for t in range(TT):
                        rows = P if t < 4 else NS
                        ins = pe.transpose(flat(s)[0:rows, t * P:(t + 1) * P], yT[s][:, t * P:t * P + rows], ident[:])
                    ins.then_inc(S["y_turned"], 1)


_INS = ['x_prompt', 'x_sample', 'cache_cmp_kv', 'cache_sel_kv', 'cache_win_kv', 'state_pool', 'page_table',
        'g_mix', 'w_in', 'pe_ck', 'w_ck1', 'w_ck2', 'pe_cv', 'w_cv1', 'w_cv2', 'w_pool_grp', 'pool_scale',
        'w_br_nsa', 'w_br_pool', 'w_o', 'g_mlp', 'w_up', 'w_down', 'g_final']
_OUTS = [(1, SEQ, D), (NB, NT, D), (1, 1, SEQ, 2, NKV, HD), (1, 1, SEQ, 2, NKV, HD), (1, 1, SEQ, 2, NKV, HD),
         (1, 1, PSTATE, PW), (1, NB, NT, 2, NKV, HD), (1, NB, NT, 2, NKV, HD), (1, NB, KEYS, 2, NKV, HD),
         (1, NB, PSTATE, PW)]


def kernel(**inputs):
    import numpy as _np
    import concourse.bacc as _bacc
    from concourse import mybir as _mybir
    from concourse.bass_utils import run_bass_kernel_spmd as _run

    nc = _bacc.Bacc("TRN2", target_bir_lowering=False, num_devices=1)
    arrays, args = {}, []
    for name in _INS:
        a = _np.ascontiguousarray(inputs[name])
        arrays[f"in_{name}_dram"] = a
        args.append(nc.dram_tensor(f"in_{name}_dram", a.shape, _mybir.dt.from_np(a.dtype), kind="ExternalInput").ap())
    for i, shape in enumerate(_OUTS):
        args.append(nc.dram_tensor(f"out_{i}_dram", shape, F32, kind="ExternalOutput").ap())
    build(nc, *args)
    r = _run(nc, [arrays], core_ids=[0])
    return tuple(r.results[0][f"out_{i}_dram"] for i in range(len(_OUTS)))
```

```python
from contextlib import ExitStack

import concourse.bass as bass
from concourse import mybir

F32 = mybir.dt.float32
F32R = mybir.dt.float32r
BF16 = mybir.dt.bfloat16
I32 = mybir.dt.int32
ALU = mybir.AluOpType
ACT = mybir.ActivationFunctionType
X = mybir.AxisListType.X

P = 128
D = 2048
KT = D // P
SEQ = 512
NB = 8
NT = 8
NS = NB * NT
TOK = SEQ + NS
HALF = TOK // 2
TT = 5
HEADS, NKV, HD = 16, 4, 64
PAST, PAGE, BLK = 256, 128, 64
PAGES = PAST // PAGE
KEYS = PAST + NT
KVC = 2 * NKV * HD
PW = 1024
PSTATE = 15
FF = 4 * D
EPS = 1e-6
NEG = -1e30
Q_COL, KV_COL, NG_COL, U_COL = 0, 1024, 1024 + 3 * KVC, 1024 + 3 * KVC + 3 * HEADS
MG_COL = U_COL + PW

C_U = 0
C_KV = C_U + 8
C_NG = C_KV + 12
C_PM = C_NG + 1
C_Q = C_PM + 1
C_MG = C_Q + 8
C_BR = C_MG + 32
C_WO = C_BR + 16
C_FF = C_WO + 16
A_X = 0
A_U = A_X + KT
A_KV = A_U + 8
A_PM = A_KV + 12
A_Q = A_PM + 8
A_MG = A_Q + 8
A_BR = A_MG + 32
A_WO = A_BR + 16
A_FF = A_WO + 16
FFG = 8
GK = FF // FFG // P
UP_PAIRS, DOWN_PAIRS = GK // 2, 4
C_GROUP = GK + 8
A_GROUP = GK + KT


def build(nc, x_prompt, x_sample, cache_cmp, cache_sel, cache_win, state_pool, page_table,
          g_mix, w_in, pe_ck, w_ck1, w_ck2, pe_cv, w_cv1, w_cv2, w_pool, pool_scale,
          w_nsa, w_bpool, w_o, g_mlp, w_up, w_down, g_final,
          y_p, y_s, p_cmp, p_sel, p_win, p_pool, s_cmp, s_sel, s_win, s_pool):
    def dram(name, shape):
        return nc.dram_tensor(name, shape, F32, kind="Internal").ap()

    qT_d = dram("qT_scratch", [8, P, TOK])
    kvT_d = dram("kvT_scratch", [12, P, TOK])
    kv_d = dram("kv_scratch", [TOK, 3 * KVC])
    gate_d = dram("gate_scratch", [NS, 3 * HEADS])
    mg_d = dram("mg_scratch", [32, P, TOK])
    kc_d = dram("kcmp_scratch", [NKV, HD, 40])
    vc_d = dram("vcmp_scratch", [NKV, 40, HD])

    with ExitStack() as ctx:
        arena = ctx.enter_context(nc.sbuf_tensor("arena", [P, 53200], F32))
        base = (nc.sbuf_base - 53200 * 4) // 32 * 32
        del arena

        def at(name, shape, offset, dt=F32):
            return nc.alloc_sbuf_tensor_at(name, shape, dt, offset=base + offset)

        def sem(name):
            return ctx.enter_context(nc.semaphore(name))

        RX, RM, RW, RE = 0, 73728, 147456, 196608
        A_hi = at("movA_hi", [P, KT, TOK], RX, F32R)
        A_lo = at("movA_lo", [P, KT, TOK], RX + 36864, F32R)
        B_hi = at("movB_hi", [P, KT, TOK], RM, F32R)
        B_lo = at("movB_lo", [P, KT, TOK], RM + 36864, F32R)
        x2T = at("x2T", [P, KT, TOK], RX)
        F_hi = at("ffn_hi", [P, GK, TOK], RX + 36864, F32R)
        F_lo = at("ffn_lo", [P, GK, TOK], RX + 55296, F32R)
        raw = [at(f"raw{s}", [P, KT * P], RW + 8192 * s) for s in range(2)]
        w_hi = [at(f"w_hi{s}", [P, KT * P], RW + 16384 + 16384 * s, F32R) for s in range(2)]
        w_lo = [at(f"w_lo{s}", [P, KT * P], RW + 24576 + 16384 * s, F32R) for s in range(2)]
        xn = at("xn", [P, TT, D], RM)
        junk = at("junk", [P, D], RM + 40960)
        stN = at("stN", [NB * PSTATE, PW], RM + 49152)
        stT = at("stT", [P, 8, NB * PSTATE], RM + 53248)
        uT = at("uT", [P, 8, TOK], RM)
        dT = at("dT", [P, 8, TOK], RM + 18432)
        PADW = 16
        wa = [at(f"win_sum{s}", [P, PADW + SEQ], RM + 57344 + 2112 * s) for s in range(2)]
        sa = [at(f"win_sum_s{s}", [P, NB, PSTATE + NT], RM + 61568 + 736 * s) for s in range(2)]
        D_hi = at("d_hi", [P, 8, TOK], RM + 36864, F32R)
        D_lo = at("d_lo", [P, 8, TOK], RM + 55296, F32R)
        unat = at("unat", [79, PW], RM + 63488)
        oP = at("oP", [P, 8, TOK], RM + 18432)
        oN = at("oN", [P, 8, TOK], RM)
        NROW = 21
        crow = at("crow", [P, NROW, NKV, HD], RM + 36864)
        w1 = [at(f"w1_{s}", [P, 16, P], RM + 8192 * s) for s in range(2)]

        G = at("cmp_hidden", [P, NKV, 20, 2], RM + 16384)
        kcs = at("kcs", [HD, NKV, 40], RM + 17024)
        w2 = [at(f"w2_{j}", [P, HD], RM + 17664 + 256 * j) for j in range(2)]
        peb = at("peb", [P, 1], RM + 18176)
        vcs = at("vcs", [40, NKV, HD], RM + 58368)
        RA = RM + 36864
        KTp = at("KTp", [HD, 2, SEQ], RA)
        Vp = at("Vp", [P, 2, 4, HD], RA + 4096)
        qh = at("qh", [HD, 2, SEQ], RA + 6144)
        kch = at("kch", [HD, 8], RA + 10240)
        vch = at("vch", [8, HD], RA + 10272)
        Pb = [at(f"Pb{j}", [P, 2, SEQ], RA + 10528 + 4096 * j) for j in range(2)]
        PTb = [at(f"PTb{j}", [P, SEQ], RA + 18720 + 2048 * j) for j in range(2)]
        kvp = at("kvp", [P, 2, PAGES, KVC], RA + 22816)
        vnew = at("vnew", [NT, 2, NKV * HD], RA + 31008)
        qz = at("qz", [P, NKV, 4, NT], RA + 33056)
        Ps = at("Ps", [P, 2, KEYS], RA + 33568)
        kc4 = at("kc4", [P, 2, 4], RA + 35680)
        pcs = at("pcs", [P, 4, 8], RA + 35712)
        pcm = at("pcm", [P, 4, 8], RA + 35840)
        pcT = at("pcT", [8, SEQ], RE + 13888)
        pc4 = at("pc4", [P, 4], RA + 35968)
        pcT4 = at("pcT4", [4, P], RA + 36000)
        nmc, rsc, wc = (at(f"cstat{j}", [P, 4], RA + 36512 + 32 * j) for j in range(3))
        nmx, rsx, wx = (at(f"pstat{j}", [P, 2, 2], RA + 36608 + 32 * j) for j in range(3))
        nms, rss, wsm = (at(f"sstat{j}", [P, 4], RA + 36704 + 32 * j) for j in range(3))

        off = [RE]

        def small(name, shape, dt=F32):
            n = 2 if dt == BF16 else 4
            for q in shape[1:]:
                n *= q
            o = off[0]
            off[0] += (n + 31) // 32 * 32
            assert off[0] <= 53200 * 4, name
            return at(name, shape, o, dt)

        ident = small("ident", [P, P])
        identb = small("identb", [P, P], BF16)
        onesm = small("ones", [P, P])
        cmask = small("cmask", [P, P], BF16)
        smask = small("smask", [P, NT], BF16)
        bmask = small("bmask", [P, 4, 8])
        vis = small("vis", [P, 4])
        gmix, gmlp, gfin = (small(n, [P, KT]) for n in ("gmix", "gmlp", "gfin"))
        psc = small("psc", [P, 8])
        gp = small("gp", [P, 4, 3 * HEADS])
        gn = small("gn", [NS, 3 * HEADS])
        gs = small("gs", [P, NB, 3])
        rc = small("rc", [P, 4, 16])
        st5 = [small(f"stat{j}", [P, 8]) for j in range(4)]
        last_mask = small("last_mask", [1, 8])
        pt = small("pt", [1, NB * PAGES], I32)
        RT = off[0]
        zT = [small(f"zT{s}", [P, TOK]) for s in range(2)]
        RN = off[0]
        zn = [small(f"zn{s}", [P, TT, P]) for s in range(2)]
        assert RN + 5248 <= RE + 13888
        KTs = at("KTs", [P, 2, 2, KEYS], RN)
        vc4 = at("vc4", [4, NKV, HD], RN + 4224)
        gateT = at("gateT", [3 * HEADS, TOK], RN)
        xr = [at(f"xr{s}", [P, TT, P], RN + 2560 * s) for s in range(2)]
        mgl = [at(f"mgl{s}", [P, 2, TOK], RT + 4608 * s) for s in range(2)]
        sq = [at(f"sq{s}", [P, TOK], RT + 2304 * s) for s in range(2)]
        rB = at("rB", [P, TOK], RN)
        tB = at("tB", [P, TOK], RN + 2304)
        ff = [at(f"ff{s}", [P, TOK], RT + 2304 * s) for s in range(2)]
        ff2 = [at(f"ff2_{s}", [P, TOK], RN + 2304 * (s + 1)) for s in range(2)]
        yT = [at(f"yT{s}", [P, TOK], RM + 2304 * s) for s in range(4)]
        yn = [at(f"yn{s}", [P, TT, P], RM + 16384 + 2560 * s) for s in range(4)]
        rF = at("rF", [P, TOK], RM + 28672)
        tF = at("tF", [P, TOK], RM + 30976)

        PS = ctx.enter_context(nc.psum_tensor("PS", [P, 8, 512], F32))

        def acc(slot, n=2):
            return PS[:, n * slot:n * slot + n, 0:HALF]

        def flat(slot):
            return PS[:, 2 * slot:2 * slot + 2, :].rearrange("p b n -> p (b n)")[:, 0:TT * P]

        def x_slot(k):
            return flat((0, 1, 3)[k % 3])

        def halves(t2d):
            return t2d.rearrange("p (h n) -> p h n", h=2)

        names = """x_loaded0 x_loaded1 x_loaded2 x_loaded3 x_loaded4 small_loaded state_loaded consts_ready masks_ready
            sq_done rstd_step rc_done stats_set x_scaled x_hi st_ready st_copied
            raw_full0 raw_full1 split_hi split_lo acc_ready acc_free
            zT_stored0 zT_stored1 nat_ready0 nat_ready1 zn_done0 zn_done1 zn_stored0 zn_stored1
            out_stored tail_stored chain_p pooled chain_v chain_a tail_ready
            ng_ready gate_exp gateT_done ng_turned gates_done gn_stored gs_loaded d_high d_ready
            crow_loaded w1_loaded0 w1_loaded1 w1_used w2_loaded pe_out gelu_done c2_ready c2_done
            kc_stored
            smp_loaded head_loaded smask_built half_full0 half_full1 chain_att br_sum A_split h_ready bank7_free
            KT_ready KT_copied ss_ready smax_done sexp_done sP_ready sPT_ready sPT_copied so_ready
            cs_ready cmask_done cexp_done cP_ready cPT_ready cPT_copied
            s_ready max_done exp_done P_ready PT_ready PT_copied pv_done
            mg_exp mg_done
            A_high merged x_turned xT_copied mg_loaded0 mg_loaded1 br_high xr_loaded0 xr_loaded1
            sq_ready sq_used root_in root_done h_high ff_squared ff_high ff_ready
            yT_scaled y_turned yn_done yn_stored0 yn_stored1 yn_stored2 yn_stored3""".split()
        S = {n: sem(n) for n in names}
        raw_full = [S["raw_full0"], S["raw_full1"]]
        SMP_DMAS, HEAD_DMAS = 13, 8
        CHAIN_SMP, CHAIN_HEAD = 3, 13

        w_in_v = w_in[0].rearrange("(k p) n -> p k n", p=P)
        block = ctx.enter_context(nc.Block())

        @block.sync
        def _(sp):
            def load(slot, src):
                sp.dma_start(raw[slot][:].rearrange("p (k n) -> p k n", n=P), src).then_inc(raw_full[slot], 16)

            def load_in(slot, col):
                load(slot, w_in_v[:, :, bass.ds(col, P)])

            for t in range(4):
                sp.dma_start(xn[:, t, :], x_prompt[0, t * P:(t + 1) * P, :]).then_inc(S[f"x_loaded{t}"], 16)
            sp.dma_start(xn[0:NS, 4, :], x_sample.rearrange("b t d -> (b t) d")).then_inc(S["x_loaded4"], 16)
            load_in(0, U_COL)
            load_in(1, U_COL + P)
            with sp.Fori(0, 3) as i:
                for s in range(2):
                    sp.wait_ge(S["split_lo"], C_U + 2 * i + s + 1)
                    load_in(s, U_COL + P * (2 * i + s + 2))
            for s in range(2):
                sp.wait_ge(S["split_lo"], C_U + 6 + s + 1)
                load_in(s, KV_COL + P * s)

            for s in range(2):
                sp.wait_ge(S[f"zn_done{s}"], 1)
            sp.dma_start(p_pool[0, 0], unat[0:PSTATE, :]).then_inc(S["tail_stored"], 16)
            sp.dma_start(s_pool[0, :, PSTATE - NT:PSTATE, :], unat[PSTATE:79, :]).then_inc(S["tail_stored"], 16)
            sp.dma_start(s_pool[0, :, 0:PSTATE - NT, :], state_pool[0, :, NT:PSTATE, :]).then_inc(S["out_stored"], 16)
            def kv_pair(i, last=False):
                for s in range(2):
                    sp.wait_ge(S["split_lo"], C_KV + 2 * i + s + 1)
                    if last and s == 1:
                        sp.dma_start(raw[s][:].rearrange("p (g c n) -> p g c n", g=4, c=2),
                                     w_pool[0].rearrange("g (c p) n -> p g c n", p=P)).then_inc(raw_full[s], 16)
                    else:
                        load_in(s, KV_COL + P * (2 * i + 2 + s))
                    sp.wait_ge(S["acc_free"], A_KV + 2 * i + s + 1)
                    sp.dma_start(kvT_d[bass.ds(2 * i + s, 1)].rearrange("m p n -> p (m n)"), zT[s][:])\
                        .then_inc(S[f"zT_stored{s}"], 16)
                for s in range(2):
                    col = P * (2 * i + s)
                    sp.wait_ge(S[f"zn_done{s}"], 2 * i + 3)
                    sp.dma_start(kv_d[0:SEQ, bass.ds(col, P)].rearrange("(t p) n -> p t n", p=P), zn[s][:, 0:4, :])\
                        .then_inc(S[f"zn_stored{s}"], 16)
                    sp.dma_start(kv_d[SEQ:TOK, bass.ds(col, P)], zn[s][0:NS, 4, :]).then_inc(S[f"zn_stored{s}"], 16)

            with sp.Fori(0, 5) as i:
                kv_pair(i)
            kv_pair(5, last=True)

            def weights(slot, n, src, dst=None):
                sp.wait_ge(S["split_lo"], n - 1)
                sp.dma_start(raw[slot][:].rearrange("p (k n) -> p k n", n=P) if dst is None else dst, src)\
                    .then_inc(raw_full[slot], 16)

            def halved_weights(s, n, upper, lower):
                sp.wait_ge(S["split_lo"], n - 1)
                w = raw[s][:].rearrange("p (k n) -> p k n", n=P)
                sp.dma_start(w[:, 0:8, :], upper).then_inc(S[f"half_full{s}"], 16)
                sp.dma_start(w[:, 8:16, :], lower).then_inc(raw_full[s], 16)

            for s in range(2):
                weights(s, C_Q + s, w_in_v[:, :, Q_COL + P * s:Q_COL + P * s + P])
            for s in range(2):
                sp.wait_ge(S[f"zn_stored{s}"], 32 * 6)
            for r, (po, so) in enumerate(((p_cmp, s_cmp), (p_sel, s_sel), (p_win, None))):
                sp.dma_start(po.rearrange("a b t c h e -> (a b t) (c h e)"), kv_d[0:SEQ, KVC * r:KVC * (r + 1)])\
                    .then_inc(S["out_stored"], 16)
                if so is not None:
                    sp.dma_start(so.rearrange("a b t c h e -> (a b t) (c h e)"), kv_d[SEQ:TOK, KVC * r:KVC * (r + 1)])\
                        .then_inc(S["out_stored"], 16)
            sw = s_win[0].rearrange("b t c h e -> b t (c h e)")
            sp.dma_start(sw[:, 0:PAST, :], cache_win[0].rearrange("b t c h e -> b t (c h e)"))\
                .then_inc(S["out_stored"], 16)
            sp.dma_start(sw[:, PAST:KEYS, :], kv_d[SEQ:TOK, 2 * KVC:].rearrange("(b t) n -> b t n", t=NT))\
                .then_inc(S["out_stored"], 16)
            def gate_weights(s, j):
                col = bass.ds(MG_COL + P * j, P)
                halved_weights(s, C_MG + j, w_in_v[:, 0:8, col], w_in_v[:, 8:16, col])

            def q_pair(i, last=False):
                for s in range(2):
                    if last:
                        gate_weights(s, s)
                    else:
                        weights(s, C_Q + 2 * i + s + 2, w_in_v[:, :, bass.ds(Q_COL + P * (2 * i + s + 2), P)])
                    sp.wait_ge(S["acc_free"], A_Q + 2 * i + s + 1)
                    sp.dma_start(qT_d[bass.ds(2 * i + s, 1)].rearrange("m p n -> p (m n)"), zT[s][:])\
                        .then_inc(S[f"zT_stored{s}"], 16)

            with sp.Fori(0, 3) as i:
                q_pair(i)
            q_pair(3, last=True)
            sp.wait_ge(S["gates_done"], 1)
            sp.dma_start(gate_d, gn[:]).then_inc(S["gn_stored"], 16)
            sp.wait_ge(S["gn_stored"], 16)
            for r in range(3):
                for n in range(HEADS):
                    sp.dma_start(gs[NT * n:NT * n + NT, :, r], gate_d[:, 16 * r + n].rearrange("(b t) -> t b", t=NT),
                                 allow_slow_non_contiguous=True).then_inc(S["gs_loaded"], 16)

            nsa_v = w_nsa[0].rearrange("(k p) n -> p k n", p=P)
            bpool_v = w_bpool[0].rearrange("(k p) n -> p k n", p=P)

            def branch_weights(s, j):
                col = bass.ds(P * j, P)
                halved_weights(s, C_BR + j, nsa_v[:, :, col], bpool_v[:, :, col])

            def mg_pair(i, last=False):
                for s in range(2):
                    if last:
                        branch_weights(s, s)
                    else:
                        gate_weights(s, 2 * i + s + 2)
                for s in range(2):
                    sp.wait_ge(S["mg_done"], 2 * i + s + 1)
                    sp.dma_start(mg_d[bass.ds(2 * i + s, 1)].rearrange("m p n -> p (m n)"), zT[s][:])\
                        .then_inc(S[f"zT_stored{s}"], 16)

            with sp.Fori(0, 15) as i:
                mg_pair(i)
            mg_pair(15, last=True)
            with sp.Fori(0, 7) as i:
                for s in range(2):
                    branch_weights(s, 2 * i + s + 2)
            wo_v = w_o[0].rearrange("(k p) n -> p k n", p=P)
            with sp.Fori(0, 8) as i:
                for s in range(2):
                    weights(s, C_WO + 2 * i + s, wo_v[:, :, bass.ds(P * (2 * i + s), P)])
            up_v = w_up[0].rearrange("(k p) n -> p k n", p=P)
            down_v = w_down[0].rearrange("(g k p) n -> p g k n", p=P, k=GK)
            with sp.Fori(0, FFG) as g:
                with sp.Fori(0, UP_PAIRS) as i:
                    for s in range(2):
                        weights(s, C_FF + C_GROUP * g + 2 * i + s, up_v[:, :, bass.ds(GK * P * g + P * (2 * i + s), P)])
                with sp.Fori(0, DOWN_PAIRS) as i:
                    for s in range(2):
                        weights(s, C_FF + GK + C_GROUP * g + 2 * i + s,
                                down_v[:, bass.ds(g, 1), :, bass.ds(256 * (2 * i + s), 256)]
                                .rearrange("p g k n -> p (g k) n"),
                                raw[s][:].rearrange("p (k n) -> p k n", n=256))
            def y_quad(i):
                for s in range(4):
                    sp.wait_ge(S["yn_done"], 8 * i + 2 * s + 2)
                    col = bass.ds(P * (4 * i + s), P)
                    sp.dma_start(y_p[0].rearrange("(t p) n -> p t n", p=P)[:, :, col], yn[s][:, 0:4, :])\
                        .then_inc(S[f"yn_stored{s}"], 16)
                    sp.dma_start(y_s.rearrange("b t n -> (b t) n")[:, col], yn[s][0:NS, 4, :])\
                        .then_inc(S[f"yn_stored{s}"], 16)

            with sp.Fori(0, 4) as i:
                y_quad(i)
            for s in range(4):
                sp.wait_ge(S[f"yn_stored{s}"], 32 * 4)
            sp.wait_ge(S["out_stored"], 16 * 8)

        @block.gpsimd
        def _(pool):
            n = [0]

            def seq(ins):
                n[0] += 1
                ins.then_inc(S["chain_p"], 1)
                pool.wait_ge(S["chain_p"], n[0])

            for st in st5:
                ins = pool.memset(st[:], 1.0)
            ins.then_inc(S["stats_set"], 1)
            seq(pool.memset(ident[:], 0.0))
            seq(pool.affine_select(out=ident[:], in_=ident[:], compare_op=ALU.not_equal, fill=1.0, base=0,
                                   pattern=[[-1, P]], channel_multiplier=1))
            seq(pool.memset(identb[:], 0.0))
            seq(pool.affine_select(out=identb[:], in_=identb[:], compare_op=ALU.not_equal, fill=1.0, base=0,
                                   pattern=[[-1, P]], channel_multiplier=1))
            pool.memset(onesm[:], 1.0).then_inc(S["consts_ready"], 1)
            for src, dst in ((g_mix, gmix), (g_mlp, gmlp)):
                pool.dma_start(dst[:], src[0].rearrange("(k p) -> p k", p=P),
                               allow_slow_non_contiguous=True).then_inc(S["small_loaded"], 16)
            pool.dma_start(gfin[:], g_final.rearrange("(k p) -> p k", p=P),
                               allow_slow_non_contiguous=True).then_inc(S["small_loaded"], 16)
            pool.dma_start(psc[:], pool_scale[0].rearrange("(k p) -> p k", p=P),
                               allow_slow_non_contiguous=True).then_inc(S["small_loaded"], 16)
            pool.dma_start(pt[:], page_table.rearrange("b n -> (b n)").unsqueeze(0),
                               allow_slow_non_contiguous=True).then_inc(S["small_loaded"], 16)
            pool.dma_start(stN[:], state_pool[0].rearrange("b r c -> (b r) c")).then_inc(S["state_loaded"], 16)
            seq(pool.memset(cmask[:], 0.0))
            seq(pool.affine_select(out=cmask[:], in_=cmask[:], compare_op=ALU.is_ge, fill=NEG, base=0,
                                   pattern=[[-1, P]], channel_multiplier=1))
            seq(pool.memset(bmask[:], 0.0))
            seq(pool.affine_select(out=bmask[:], in_=bmask[:], compare_op=ALU.is_ge, fill=NEG, base=-(BLK - 1),
                                   pattern=[[P, 4], [-BLK, 8]], channel_multiplier=1))
            seq(pool.memset(vis[:], 1.0))
            seq(pool.affine_select(out=vis[:], in_=vis[:], compare_op=ALU.is_ge, fill=0.0, base=-(BLK - 1),
                                   pattern=[[P, 4]], channel_multiplier=1))
            for t in range(16):
                ins = pool.memset(rc[:, 0, t:t + 1], float(t + 1))
            seq(ins)
            for g in (3, 2, 1):
                seq(pool.tensor_scalar(rc[:, g, :], rc[:, 0, :], float(2 << g), None, ALU.min))
            seq(pool.tensor_scalar(rc[:, 0, :], rc[:, 0, :], 2.0, None, ALU.min))
            for w in wa:
                seq(pool.memset(w[:, 0:PADW], 0.0))
            for j in range(HEADS):
                pool.dma_start(smask[NT * j:NT * j + NT], cmask[0:NT, 0:NT]).then_inc(S["smask_built"], 16)
            pool.wait_ge(S["smask_built"], 16 * HEADS)
            pool.memset(last_mask[:], 0.0).then_inc(S["masks_ready"], 1)

            pool.wait_ge(S["st_copied"], 1)
            pool.wait_ge(S["rc_done"], 1)
            for m in range(8):
                g = m // 2
                pool.wait_ge(S["acc_free"], A_U + m + 1)
                us = uT[:, m, SEQ:TOK].rearrange("p (b t) -> p b t", t=NT)
                pool.tensor_copy(wa[0][:, PADW:], uT[:, m, 0:SEQ])
                pool.tensor_copy(sa[0][:, :, 0:PSTATE], stT[:, m, :].rearrange("p (b r) -> p b r", r=PSTATE))
                seq(pool.tensor_copy(sa[0][:, :, PSTATE:], us))
                for k in range(g + 1):
                    a, b, sh = k % 2, 1 - k % 2, 1 << k
                    lo = 2 * sh - 1
                    pool.tensor_tensor(wa[b][:, PADW:], wa[a][:, PADW:], wa[a][:, PADW - sh:PADW + SEQ - sh], ALU.add)
                    seq(pool.tensor_tensor(sa[b][:, :, lo:], sa[a][:, :, lo:], sa[a][:, :, lo - sh:PSTATE + NT - sh],
                                           ALU.add))
                r = (g + 1) % 2
                iw = 1.0 / (2 << g)
                pool.tensor_tensor(wa[1 - r][:, PADW:PADW + 16], wa[r][:, PADW:PADW + 16], rc[:, g, :], ALU.mult)
                pool.tensor_scalar(wa[1 - r][:, PADW + 16:], wa[r][:, PADW + 16:], iw, None, ALU.mult)
                seq(pool.tensor_scalar(sa[1 - r][:, :, PSTATE:], sa[r][:, :, PSTATE:], iw, None, ALU.mult))
                pool.tensor_tensor(dT[:, m, 0:SEQ], wa[1 - r][:, PADW:], uT[:, m, 0:SEQ], ALU.subtract)
                pool.tensor_tensor(dT[:, m, SEQ:TOK].rearrange("p (b t) -> p b t", t=NT), sa[1 - r][:, :, PSTATE:], us,
                                   ALU.subtract).then_inc(S["pooled"], 1)
                pool.wait_ge(S["pooled"], m + 1)

            w1c = [w[0].rearrange("(s d) n -> s d n", d=HD) for w in (w_ck1, w_cv1)]
            pool.wait_ge(S["tail_ready"], 1)
            pool.dma_start(w2[0][:], w_ck2[0]).then_inc(S["w2_loaded"], 16)
            pool.dma_start(w2[1][:], w_cv2[0]).then_inc(S["w2_loaded"], 16)

            def w1_load(c):
                s, kv, q = c % 2, c // 4, c % 4
                if c >= 2:
                    pool.wait_ge(S["w1_used"], c - 1)
                for h in range(2):
                    pool.dma_start(w1[s][64 * h:64 * h + 64], w1c[kv][:, 16 * q:16 * q + 16, :])\
                        .then_inc(S[f"w1_loaded{s}"], 16)

            w1_load(0)
            w1_load(1)
            for kv, pe_ in enumerate((pe_ck, pe_cv)):
                if kv == 0:
                    pool.wait_ge(S["acc_ready"], A_PM + 8)
                    for s in range(2):
                        pool.wait_ge(S[f"zn_stored{s}"], 32 * 6)
                else:
                    pool.wait_ge(S["w1_used"], 4)
                cols = slice(4 * HD * kv, 4 * HD * kv + 4 * HD)
                pool.dma_start(crow[:, 0:4].rearrange("p t h e -> p t (h e)"),
                               kv_d[0:SEQ, cols].rearrange("(t p) n -> p t n", p=P)).then_inc(S["crow_loaded"], 16)
                pool.dma_start(crow[0:BLK, 20, 0, :], pe_[0]).then_inc(S["crow_loaded"], 16)
                with pool.Fori(0, NB * PAGES) as j:
                    page = pool.value_load(pt[0:1, bass.ds(j, 1)], min_val=0, max_val=cache_cmp.shape[1] - 1)
                    pool.dma_start(crow[:, bass.ds(4 + j, 1)].rearrange("p t h e -> p (t h e)"),
                                   cache_cmp[0][bass.ds(page, 1), :, kv].rearrange("g s h e -> s (g h e)"))\
                        .then_inc(S["crow_loaded"], 16)
                for c in range(4 * kv + 2, min(4 * kv + 6, 8)):
                    w1_load(c)

            pool.wait_ge(S["c2_done"], 1)
            pool.dma_start(kc_d.rearrange("h e b -> e h b"), kcs[:]).then_inc(S["kc_stored"], 16)
            pool.wait_ge(S["c2_done"], 2)
            pool.dma_start(vc_d.rearrange("h b e -> b h e"), vcs[:]).then_inc(S["kc_stored"], 16)
            pool.wait_ge(S["kc_stored"], 32)
            for t in range(2):
                pool.wait_ge(S[f"zT_stored{t}"], 160)
            kvT_h = kvT_d.rearrange("m (e d) t -> (m e) d t", e=2)
            qT_h = qT_d.rearrange("m (e d) t -> (m e) d t", e=2)

            def sample_loads(b, first=False):
                def ld(dst, src):
                    pool.dma_start(dst, src).then_inc(S["smp_loaded"], 16)

                if not first:
                    pool.wait_ge(S["so_ready"], b)
                new = bass.ds(SEQ + NT * b, NT)
                for g in range(PAGES):
                    page = pool.value_load(pt[0:1, bass.ds(PAGES * b + g, 1)], min_val=0, max_val=cache_sel.shape[1] - 1)
                    ld(kvp[:, 0, g, :], cache_sel[0][bass.ds(page, 1)].rearrange("g s c h e -> s (g c h e)"))
                ld(kvp[:, 1], cache_win[0][bass.ds(b, 1)].rearrange("b (g s) c h e -> s (b g) (c h e)", s=P))
                ld(vnew[:], kv_d[new, KVC:].rearrange("t (r c n) -> t r c n", r=2, c=2)[:, :, 1, :])
                for r in range(2):
                    ld(KTs[:, r, :, PAST:], kvT_d[4 * (r + 1):4 * (r + 1) + 2, :, new].rearrange("c p t -> p c t"))
                for e in range(2):
                    for c in range(2):
                        h = 2 * c + e
                        ld(qz[64 * e:64 * e + 64, h], qT_h[4 * h:4 * h + 4, :, new].rearrange("g d t -> d g t"))
                    ld(kc4[64 * e:64 * e + 64], kc_d.rearrange("(c e) d b -> e d c b", e=2)[e][:, :, bass.ds(8 + 4 * b, 4)])
                ld(vc4[:], vc_d[:, bass.ds(8 + 4 * b, 4), :].rearrange("h b e -> b h e"))

            def head_loads(i, first=False):
                def ld(dst, src):
                    pool.dma_start(dst, src).then_inc(S["head_loaded"], 16)

                if not first:
                    pool.wait_ge(S["pv_done"], 16 * i)
                h = i // 2
                for r in range(2):
                    ld(KTp[:, r, :], kvT_h[bass.ds(8 * (r + 1) + h, 1), :, 0:SEQ].rearrange("m d t -> d (m t)"))
                    ld(Vp[:, r], kv_d[0:SEQ, bass.ds(KVC * (r + 1) + 4 * HD + HD * h, HD)]
                       .rearrange("(t p) e -> p t e", p=P))
                    ld(qh[:, r, :], qT_h[bass.ds(2 * i + r, 1), :, 0:SEQ].rearrange("m d t -> d (m t)"))
                ld(kch[:], kc_d[bass.ds(h, 1), :, 0:8].rearrange("h d b -> d (h b)"))
                ld(vch[:], vc_d[bass.ds(h, 1), 0:8, :].rearrange("h b e -> (h b) e"))

            seq(pool.memset(qz[:], 0.0))
            sample_loads(0, first=True)
            head_loads(0, first=True)
            with pool.Fori(1, NB) as i:
                sample_loads(i)
                head_loads(i)

            for s in range(2):
                pool.wait_ge(S[f"zT_stored{s}"], 160 + 16 * 16)

            def mg_loads(i, first=False):
                for s in range(2):
                    if not first:
                        pool.wait_ge(S["merged"], 2 * i + s - 1)
                    for j in range(2):
                        pool.dma_start(mgl[s][:, j, :], mg_d[bass.ds(16 * j + 2 * i + s, 1)].rearrange("m p n -> p (m n)"))\
                            .then_inc(S[f"mg_loaded{s}"], 16)

            mg_loads(0, first=True)
            with pool.Fori(1, 8) as i:
                mg_loads(i)

            def x_loads(i, first=False):
                for s in range(2):
                    if first:
                        pool.wait_ge(S["merged"], 16)
                    else:
                        pool.wait_ge(S["x_turned"], 2 * i + s - 1)
                    col = bass.ds(P * (2 * i + s), P)
                    pool.dma_start(xr[s][:, 0:4, :], x_prompt[0].rearrange("(t p) n -> p t n", p=P)[:, :, col])\
                        .then_inc(S[f"xr_loaded{s}"], 16)
                    pool.dma_start(xr[s][0:NS, 4, :], x_sample.rearrange("b t n -> (b t) n")[:, col])\
                        .then_inc(S[f"xr_loaded{s}"], 16)

            x_loads(0, first=True)
            with pool.Fori(1, 8) as i:
                x_loads(i)

        @block.scalar
        def _(act):
            def hi(pair, slot, before=None):
                act.wait_ge(raw_full[slot], 16 * pair + 16)
                if before is not None:
                    act.wait_ge(S["acc_ready"], before)
                act.activation(w_hi[slot][:], raw[slot][:], ACT.Copy).then_inc(S["split_hi"], 1)

            act.wait_ge(S["stats_set"], 1)
            for t in range(TT):
                rows = P if t < 4 else NS
                act.wait_ge(S[f"x_loaded{t}"], 16)
                if t:
                    act.wait_ge(S["sq_done"], t)
                act.activation(junk[0:rows], xn[0:rows, t, :], ACT.Square, accum_out=st5[0][0:rows, t:t + 1])\
                    .then_inc(S["sq_done"], 1)
            act.wait_ge(S["rstd_step"], 1)
            act.activation(st5[2][:, 0:TT], st5[1][:, 0:TT], ACT.Sqrt).then_inc(S["chain_a"], 1)
            hi(0, 0)
            act.wait_ge(S["small_loaded"], 80)
            for k in range(KT):
                act.wait_ge(S["acc_ready"], A_X + k + 1)
                act.activation(A_hi[:, k, :], x_slot(k)[:, 0:TOK], ACT.Copy, scale=gmix[:, k:k + 1])\
                    .then_inc(S["x_hi"], 1)
            with act.Fori(0, 4) as i:
                for s in range(2):
                    hi(C_U // 2 + i + s, 1 - s, A_U + 2 * i + s)
            with act.Fori(0, 6) as i:
                for s in range(2):
                    hi(C_KV // 2 + i + s, 1 - s, A_KV + 2 * i + s)
            act.wait_ge(S["pooled"], 8)
            act.wait_ge(S["tail_stored"], 32)
            act.activation(D_hi[:], dT[:], ACT.Copy).then_inc(S["d_high"], 1)
            hi(C_PM // 2, 1, A_PM)
            act.wait_ge(S["ng_ready"], 1)
            act.wait_ge(S["zn_stored0"], 192)
            act.activation(halves(gateT[:]), acc(3)[0:3 * HEADS], ACT.Exp, scale=-1.0)\
                .then_inc(S["gate_exp"], 1)
            hi(C_Q // 2, 0)

            def q_pair(i):
                for s in range(2):
                    j = 2 * i + s
                    if j == 7:
                        act.wait_ge(S["half_full0"], 16)
                    hi(C_Q // 2 + i + s, 1 - s, A_Q + j)

            def hidden(kv):
                act.wait_ge(S["w1_used"], 4 * kv + 4)
                if kv:
                    act.wait_ge(S["c2_ready"], 1)
                act.activation(peb[:], PS[:, 4, 80:81], ACT.Copy).then_inc(S["pe_out"], 1)
                act.wait_ge(S["pe_out"], kv + 1)
                for half in range(2):
                    act.activation(G[:, :, :, half].rearrange("p h t -> p t h"),
                                   PS[:, 4 + half, 0:80].rearrange("p (t h) -> p t h", h=NKV),
                                   ACT.Gelu_apprx_tanh, bias=peb[:]).then_inc(S["gelu_done"], 1)

            q_pair(0)
            q_pair(1)
            hidden(0)
            q_pair(2)
            q_pair(3)
            act.wait_ge(S["half_full1"], 16)
            hi(C_MG // 2, 1, A_MG)
            hidden(1)

            def gate_step(i, m):
                s, pair = m % 2, 2 * i + m // 2 + 1
                act.wait_ge(S["acc_ready"], A_MG + 4 * i + m + 1)
                act.wait_ge(S[f"zT_stored{s}"], 160 + 16 * (2 * i + m // 2))
                act.activation(halves(zT[s][:]), acc(s), ACT.Exp, scale=-1.0).then_inc(S["mg_exp"], 1)
                act.wait_ge(S[f"half_full{s}"], 16 * pair + 16)
                hi(C_MG // 2 + pair, s)

            def sample(b):
                act.wait_ge(S["KT_ready"], b + 1)
                act.activation(KTs[:, :, :, 0:PAST], PS[:, 4:6, :].rearrange("p r (c n) -> p r c n", c=2), ACT.Copy)\
                    .then_inc(S["KT_copied"], 1)
                act.wait_ge(S["smax_done"], b + 1)
                act.activation(pc4[:], PS[:, 6, 0:4], ACT.Exp, bias=nms[:, 0:1], accum_out=rss[:, 0:1])\
                    .then_inc(S["sexp_done"], 1)
                for r in range(2):
                    act.activation(Ps[:, r, :], PS[:, 4 + r, 0:KEYS], ACT.Exp, bias=nms[:, r + 1:r + 2],
                                   accum_out=rss[:, r + 1:r + 2]).then_inc(S["sexp_done"], 1)
                for r in range(2):
                    act.wait_ge(S["sPT_ready"], 2 * b + r + 1)
                    if r == 0:
                        act.activation(pcT4[:], PS[0:4, 6, 384:512], ACT.Copy)
                    act.activation(PTb[r][0:NT, 256:384], PS[0:NT, 6, 256:384], ACT.Copy)
                    act.activation(PTb[r][:, 0:256], PS[:, 6, 0:256], ACT.Copy).then_inc(S["sPT_copied"], 1)

            def head(i, par):
                def exps(t):
                    act.wait_ge(S["max_done"], 8 * i + 4 * par + t + 1)
                    for r in range(2):
                        act.activation(Pb[t % 2][:, r, 0:P * (t + 1)], PS[:, 4 + r, 0:P * (t + 1)], ACT.Exp,
                                       bias=nmx[:, t % 2, r:r + 1], accum_out=rsx[:, t % 2, r:r + 1])\
                            .then_inc(S["exp_done"], 1)

                def turned(k):
                    act.wait_ge(S["PT_ready"], 16 * i + 8 * par + k + 1)
                    n = P * (k // 2 + 1)
                    act.activation(PTb[k % 2][:, 0:n], PS[:, 6, 0:n], ACT.Copy).then_inc(S["PT_copied"], 1)

                act.wait_ge(S["cmask_done"], 2 * i + par + 1)
                act.activation(pcm[:], pcs[:], ACT.Exp).then_inc(S["cexp_done"], 1)
                exps(0)
                act.wait_ge(S["cPT_ready"], 2 * i + par + 1)
                act.activation(pcT[:], PS[0:8, 6, :], ACT.Copy).then_inc(S["cPT_copied"], 1)
                exps(1)
                turned(0)
                turned(1)
                exps(2)
                turned(2)
                turned(3)
                exps(3)
                turned(4)
                gate_step(i, 2 if par else 1)
                for k in range(5, 8):
                    turned(k)
                if par:
                    gate_step(i, 3)

            with act.Fori(0, NB) as i:
                sample(i)
                gate_step(i, 0)
                head(i, 0)
                head(i, 1)

            act.wait_ge(S["acc_ready"], A_BR)
            act.wait_ge(S["bank7_free"], 2 * NB + 1)
            for k in range(KT):
                act.activation(A_hi[:, k, :], (oN if k < 8 else oP)[:, k % 8, :], ACT.Copy).then_inc(S["A_high"], 1)

            def br_pair(i, first=False, last=False):
                for s in range(2):
                    if not (first and s == 0):
                        if not (last and s == 1):
                            act.wait_ge(S[f"half_full{1 - s}"], 16 * (16 + i + s) + 16)
                        hi(C_BR // 2 + i + s, 1 - s, A_BR + 2 * i + s)
                    act.wait_ge(S["br_sum"], 2 * i + s + 1)
                    act.activation(B_hi[:, bass.ds(2 * i + s, 1), :], mgl[s][:, 0:1, :], ACT.Copy)\
                        .then_inc(S["br_high"], 1)

            br_pair(0, first=True)
            with act.Fori(1, 7) as i:
                br_pair(i)
            br_pair(7, last=True)
            def square(t, k):
                act.activation(sq[k][:].unsqueeze(1), x2T[:, bass.ds(t, 1), :], ACT.Square).then_inc(S["sq_ready"], 1)

            def wo_pair(i, first=False):
                for s in range(2):
                    j = 2 * i + s
                    hi(C_WO // 2 + i + s, 1 - s, A_WO + j)
                    if not (first and s == 0):
                        act.wait_ge(S["acc_free"], A_WO + j)
                        square(j - 1, 1 - s)

            wo_pair(0, first=True)
            with act.Fori(1, 8) as i:
                wo_pair(i)
            act.wait_ge(S["acc_free"], A_FF)
            square(KT - 1, 1)
            for k in range(KT):
                act.activation(B_hi[:, k, :], x2T[:, k, :], ACT.Copy, scale=gmlp[:, k:k + 1]).then_inc(S["h_high"], 1)
                if k == 4:
                    act.wait_ge(S["root_in"], 1)
                    act.activation(rB[:], tB[:], ACT.Sqrt).then_inc(S["root_done"], 1)

            def last_square(a0, t):
                act.wait_ge(S["acc_free"], a0 + GK + t + 1)
                act.wait_ge(S["sq_used"], KT + t - 1)
                square(t, t % 2)

            def group(g, last=False):
                c0, a0 = C_FF // 2 + C_GROUP // 2 * g, A_FF + A_GROUP * g
                with act.Fori(0, UP_PAIRS) as i:
                    for s in range(2):
                        hi(c0 + i + s, 1 - s, a0 + 2 * i + s)
                        act.wait_ge(S["acc_free"], a0 + 2 * i + s + 1)
                        act.activation(F_hi[:, bass.ds(2 * i + s, 1), :].rearrange("p k n -> p (k n)"), ff[s][:],
                                       ACT.Square).then_inc(S["ff_high"], 1)

                def down(i):
                    for s in range(2):
                        hi(c0 + UP_PAIRS + i + s, 1 - s, a0 + GK + 4 * i + 2 * s)

                if last:
                    for i in range(DOWN_PAIRS):
                        for s in range(2):
                            if (i, s) != (DOWN_PAIRS - 1, 1):
                                hi(c0 + UP_PAIRS + i + s, 1 - s, a0 + GK + 4 * i + 2 * s)
                            if i or s:
                                for e in range(2):
                                    last_square(a0, 4 * i + 2 * s - 2 + e)
                    for e in range(2):
                        last_square(a0, KT - 2 + e)
                else:
                    with act.Fori(0, DOWN_PAIRS) as i:
                        down(i)

            with act.Fori(0, FFG - 1) as g:
                group(g)
            group(FFG - 1, last=True)
            act.wait_ge(S["root_in"], 2)
            act.activation(rF[:], tF[:], ACT.Sqrt).then_inc(S["root_done"], 1)

            def y_quad(i, first=False):
                for s in range(4):
                    act.wait_ge(S["y_turned"], 4 * i + s + 1)
                    if not first:
                        act.wait_ge(S[f"yn_stored{s}"], 32 * i)
                    act.activation(yn[s][:, 0:4, :].rearrange("p t n -> p (t n)"), flat(s)[:, 0:SEQ], ACT.Copy)\
                        .then_inc(S["yn_done"], 1)
                    act.activation(yn[s][0:NS, 4, :], flat(s)[0:NS, SEQ:], ACT.Copy).then_inc(S["yn_done"], 1)

            y_quad(0, first=True)
            with act.Fori(1, 4) as i:
                y_quad(i)

        @block.vector
        def _(dve):
            n = [0]

            def seq(ins):
                n[0] += 1
                ins.then_inc(S["chain_v"], 1)
                dve.wait_ge(S["chain_v"], n[0])

            def lo(n, slot):
                dve.wait_ge(S["split_hi"], n + 1)
                dve.tensor_tensor(w_lo[slot][:], raw[slot][:], w_hi[slot][:].bitcast(F32), ALU.subtract)\
                    .then_inc(S["split_lo"], 1)

            ss, v, r, q = (st5[j][:, 0:TT] for j in range(4))
            dve.wait_ge(S["sq_done"], TT)
            dve.tensor_scalar(v, ss, 1.0 / D, EPS, ALU.mult, ALU.add).then_inc(S["rstd_step"], 1)
            dve.wait_ge(S["chain_a"], 1)
            seq(dve.reciprocal(r, r))
            seq(dve.tensor_tensor(q, r, r, ALU.mult))
            seq(dve.tensor_tensor(q, q, v, ALU.mult))
            seq(dve.tensor_scalar(q, q, -0.5, 1.5, ALU.mult, ALU.add))
            seq(dve.tensor_tensor(r, r, q, ALU.mult))
            for t in range(TT):
                rows = P if t < 4 else NS
                dve.tensor_scalar(xn[0:rows, t, :], xn[0:rows, t, :], r[0:rows, t:t + 1], None, ALU.mult)\
                    .then_inc(S["x_scaled"], 1)
            lo(0, 0)
            dve.wait_ge(S["st_ready"], 1)
            dve.tensor_copy(stT[:].rearrange("p (h m) r -> p h (m r)", h=2), PS[:, 4:6, 0:4 * NB * PSTATE])\
                .then_inc(S["st_copied"], 1)
            for k in range(KT):
                dve.wait_ge(S["x_hi"], k + 1)
                dve.scalar_tensor_tensor(out=A_lo[:, k, :], in0=x_slot(k)[:, 0:TOK], scalar=gmix[:, k:k + 1],
                                         in1=A_hi[:, k, :].bitcast(F32), op0=ALU.mult, op1=ALU.subtract)\
                    .then_inc(S["acc_free"], 1)
            dve.wait_ge(S["masks_ready"], 1)
            dve.reciprocal(rc[:], rc[:]).then_inc(S["rc_done"], 1)
            with dve.Fori(0, 4) as i:
                for s in range(2):
                    lo(C_U + 2 * i + s + 1, 1 - s)
                    dve.wait_ge(S["acc_ready"], A_U + 2 * i + s + 1)
                    dve.tensor_copy(uT[:, bass.ds(2 * i + s, 1), :].rearrange("p m (h n) -> p (m h) n", h=2), acc(s))\
                        .then_inc(S["acc_free"], 1)
            dve.wait_ge(S["tail_ready"], 1)
            for j in range(2):
                dve.tensor_copy(unat[:, 512 * j:512 * j + 512], PS[0:79, 4 + 2 * j, :]).then_inc(S[f"zn_done{j}"], 1)

            def kv_pair(i, first=False):
                for s in range(2):
                    lo(C_KV + 2 * i + s + 1, 1 - s)
                    dve.wait_ge(S["acc_ready"], A_KV + 2 * i + s + 1)
                    if not first:
                        dve.wait_ge(S[f"zT_stored{s}"], 16 * i)
                    dve.tensor_copy(halves(zT[s][:]), acc(s)).then_inc(S["acc_free"], 1)
                for s in range(2):
                    dve.wait_ge(S[f"nat_ready{s}"], i + 1)
                    if not first:
                        dve.wait_ge(S[f"zn_stored{s}"], 32 * i)
                    dve.tensor_copy(zn[s][:, 0:4, :].rearrange("p t n -> p (t n)"), flat(2 + s)[:, 0:SEQ])\
                        .then_inc(S[f"zn_done{s}"], 1)
                    dve.tensor_copy(zn[s][0:NS, 4, :], flat(2 + s)[0:NS, SEQ:]).then_inc(S[f"zn_done{s}"], 1)

            kv_pair(0, first=True)
            with dve.Fori(1, 6) as i:
                kv_pair(i)
            dve.wait_ge(S["d_high"], 1)
            dve.tensor_tensor(D_lo[:], dT[:], D_hi[:].bitcast(F32), ALU.subtract).then_inc(S["d_ready"], 1)
            lo(C_NG + 1, 1)
            for m in range(8):
                dve.wait_ge(S["acc_ready"], A_PM + m + 1)
                dve.tensor_scalar(halves(oP[:, m, :]), acc(m % 2), psc[:, m:m + 1], None, ALU.mult)\
                    .then_inc(S["acc_free"], 1)
                if m == 3:
                    lo(C_PM + 1, 0)
            dve.wait_ge(S["gate_exp"], 1)
            seq(dve.tensor_scalar(gateT[:], gateT[:], 1.0, None, ALU.add))
            dve.reciprocal(gateT[:], gateT[:]).then_inc(S["gateT_done"], 1)
            def q_pair(i):
                for s in range(2):
                    lo(C_Q + 2 * i + s + 1, 1 - s)
                    dve.wait_ge(S["acc_ready"], A_Q + 2 * i + s + 1)
                    dve.wait_ge(S[f"zT_stored{s}"], 16 * (6 + i))
                    dve.tensor_scalar(halves(zT[s][:]), acc(s), HD ** -0.5, None, ALU.mult).then_inc(S["acc_free"], 1)

            q_pair(0)
            dve.wait_ge(S["ng_turned"], 1)
            dve.tensor_copy(gn[:], PS[0:NS, 6, 192:240]).then_inc(S["bank7_free"], 1)
            seq(dve.tensor_copy(gp[:].rearrange("p t n -> p (t n)"), PS[:, 6, 0:192]))
            dve.tensor_scalar(gp[:, 0, 0:HEADS], gp[:, 0, 0:HEADS], vis[:, 0:1], None, ALU.mult)\
                .then_inc(S["gates_done"], 1)
            q_pair(1)
            q_pair(2)
            dve.wait_ge(S["c2_ready"], 1)
            dve.tensor_copy(kcs[:].rearrange("e h b -> e (h b)"), PS[0:HD, 6, 0:160]).then_inc(S["c2_done"], 1)
            q_pair(3)
            lo(C_MG + 1, 1)
            dve.wait_ge(S["c2_ready"], 2)
            dve.tensor_copy(vcs[:].rearrange("b h e -> b (h e)"), PS[0:40, 6, 0:256]).then_inc(S["c2_done"], 1)
            dve.wait_ge(S["gs_loaded"], 16 * 48)

            def gate_step(i, m):
                s, a = m % 2, A_MG + 4 * i + m + 1
                dve.wait_ge(S["mg_exp"], 4 * i + m + 1)
                dve.tensor_scalar(zT[s][:], zT[s][:], 1.0, None, ALU.add).then_inc(S["acc_free"], 1)
                dve.wait_ge(S["acc_free"], a)
                dve.reciprocal(zT[s][:], zT[s][:]).then_inc(S["mg_done"], 1)
                lo(C_MG + 4 * i + m + 2, s)

            local = [0]

            def linked(i, ins):
                local[0] += 1
                ins.then_inc(S["chain_att"], 1)
                dve.wait_ge(S["chain_att"], (CHAIN_SMP + 2 * CHAIN_HEAD) * i + local[0])

            def sample(b):
                dve.wait_ge(S["ss_ready"], b + 1)
                dve.tensor_reduce(nms[:, 0:1], PS[:, 6, 0:4], X, ALU.max, negate=True)
                linked(b, dve.tensor_tensor(PS[:, 4:6, PAST:KEYS], PS[:, 4:6, PAST:KEYS],
                                            smask[:].unsqueeze(1).broadcast_to([P, 2, NT]), ALU.add))
                dve.tensor_reduce(nms[:, 1:3], PS[:, 4:6, 0:KEYS], X, ALU.max, negate=True).then_inc(S["smax_done"], 1)
                dve.wait_ge(S["sexp_done"], 3 * b + 3)
                linked(b, dve.reciprocal(wsm[:, 0:3], rss[:, 0:3]))
                linked(b, dve.tensor_tensor(wsm[:, 0:3].unsqueeze(1), wsm[:, 0:3].unsqueeze(1), gs[:, bass.ds(b, 1), :],
                                            ALU.mult))
                dve.tensor_scalar(pc4[:], pc4[:], wsm[:, 0:1], None, ALU.mult)
                for r in range(2):
                    dve.tensor_scalar(Ps[:, r, :], Ps[:, r, :], wsm[:, r + 1:r + 2], None, ALU.mult)\
                        .then_inc(S["sP_ready"], 1)
                gate_step(b, 0)
                dve.wait_ge(S["so_ready"], b + 1)
                dve.tensor_copy(oN[:, :, bass.ds(SEQ + NT * b, NT)], PS[:, 7, 0:64].rearrange("p (k t) -> p k t", t=NT))\
                    .then_inc(S["bank7_free"], 1)

            def head(i, par):
                def top(t):
                    dve.wait_ge(S["s_ready"], 8 * i + 4 * par + t + 1)
                    dve.tensor_reduce(nmx[:, t % 2, :], PS[:, 4:6, 0:P * (t + 1)], X, ALU.max, negate=True)\
                        .then_inc(S["max_done"], 1)

                def weigh(t):
                    dve.wait_ge(S["exp_done"], 16 * i + 8 * par + 2 * t + 2)
                    linked(i, dve.reciprocal(wx[:, t % 2, :], rsx[:, t % 2, :]))
                    g = gp[:, t, HEADS:].rearrange("p (r n) -> p r n", r=2)[:, :, bass.ds(2 * i + par, 1)]
                    linked(i, dve.tensor_tensor(wx[:, t % 2, :].unsqueeze(2), wx[:, t % 2, :].unsqueeze(2), g, ALU.mult))
                    for r in range(2):
                        part = Pb[t % 2][:, r, 0:P * (t + 1)]
                        dve.tensor_scalar(part, part, wx[:, t % 2, r:r + 1], None, ALU.mult).then_inc(S["P_ready"], 1)

                dve.wait_ge(S["cs_ready"], 2 * i + par + 1)
                linked(i, dve.tensor_tensor(pcs[:], PS[:, 6, 0:32].rearrange("p (t b) -> p t b", b=8), bmask[:], ALU.add))
                linked(i, dve.tensor_reduce(nmc[:], pcs[:], X, ALU.max))
                dve.tensor_tensor(pcs[:], pcs[:], nmc[:].unsqueeze(2).broadcast_to([P, 4, 8]), ALU.subtract)\
                    .then_inc(S["cmask_done"], 1)
                top(0)
                dve.wait_ge(S["cexp_done"], 2 * i + par + 1)
                linked(i, dve.tensor_reduce(rsc[:], pcm[:], X, ALU.add))
                linked(i, dve.reciprocal(wc[:], rsc[:]))
                linked(i, dve.tensor_tensor(wc[:].unsqueeze(2), wc[:].unsqueeze(2), gp[:, :, bass.ds(2 * i + par, 1)],
                                            ALU.mult))
                dve.tensor_tensor(pcm[:], pcm[:], wc[:].unsqueeze(2).broadcast_to([P, 4, 8]), ALU.mult)\
                    .then_inc(S["cP_ready"], 1)
                weigh(0)
                for t in range(1, 4):
                    top(t)
                    weigh(t)
                gate_step(i, 2 if par else 1)

            with dve.Fori(0, NB) as i:
                sample(i)
                head(i, 0)
                head(i, 1)
                dve.wait_ge(S["pv_done"], 16 * i + 16)
                dve.tensor_copy(oN[:, bass.ds(i, 1), 0:SEQ], PS[:, 7:8, :]).then_inc(S["bank7_free"], 1)
                gate_step(i, 3)
            assert local[0] == CHAIN_SMP + 2 * CHAIN_HEAD

            for k in range(KT):
                dve.wait_ge(S["A_high"], k + 1)
                dve.tensor_tensor(A_lo[:, k, :], (oN if k < 8 else oP)[:, k % 8, :], A_hi[:, k, :].bitcast(F32),
                                  ALU.subtract).then_inc(S["A_split"], 1)
            def br_pair(i, first=False):
                for s in range(2):
                    j = 2 * i + s
                    if not (first and s == 0):
                        lo(C_BR + j + 1, 1 - s)
                    dve.wait_ge(S["acc_ready"], A_BR + j + 1)
                    dve.wait_ge(S[f"mg_loaded{s}"], 32 * i + 32)
                    pair = acc(s, 4)
                    dve.tensor_tensor(halves(mgl[s][:, 0, :]), pair[:, 0:2, :], halves(mgl[s][:, 0, :]), ALU.mult)
                    dve.tensor_tensor(halves(mgl[s][:, 1, :]), pair[:, 2:4, :], halves(mgl[s][:, 1, :]), ALU.mult)\
                        .then_inc(S["acc_free"], 1)
                    dve.wait_ge(S["acc_free"], A_BR + j + 1)
                    dve.tensor_tensor(mgl[s][:, 0, :], mgl[s][:, 0, :], mgl[s][:, 1, :], ALU.add).then_inc(S["br_sum"], 1)
                    dve.wait_ge(S["br_high"], j + 1)
                    dve.tensor_tensor(B_lo[:, bass.ds(j, 1), :], mgl[s][:, 0:1, :],
                                      B_hi[:, bass.ds(j, 1), :].bitcast(F32), ALU.subtract).then_inc(S["merged"], 1)

            br_pair(0, first=True)
            with dve.Fori(1, 8) as i:
                br_pair(i)
            with dve.Fori(0, 8) as i:
                for s in range(2):
                    j = 2 * i + s
                    lo(C_WO + j + 1, 1 - s)
                    tile_ = x2T[:, bass.ds(j, 1), :].rearrange("p m (h n) -> p (m h) n", h=2)
                    dve.wait_ge(S["x_turned"], j + 1)
                    dve.tensor_copy(tile_, acc(2)).then_inc(S["xT_copied"], 1)
                    dve.wait_ge(S["xT_copied"], j + 1)
                    dve.wait_ge(S["acc_ready"], A_WO + j + 1)
                    dve.tensor_tensor(tile_, acc(s), tile_, ALU.add)\
                        .then_inc(S["acc_free"], 1)

            for k in range(KT):
                dve.wait_ge(S["h_high"], k + 1)
                dve.scalar_tensor_tensor(out=B_lo[:, k, :], in0=x2T[:, k, :], scalar=gmlp[:, k:k + 1],
                                         in1=B_hi[:, k, :].bitcast(F32), op0=ALU.mult, op1=ALU.subtract)\
                    .then_inc(S["h_ready"], 1)
                if k == 2:
                    dve.wait_ge(S["sq_used"], KT)
                    dve.tensor_scalar(halves(tB[:]), acc(3), 1.0 / D, EPS, ALU.mult, ALU.add).then_inc(S["root_in"], 1)

            def inverse_root(k, r, v, t):
                dve.wait_ge(S["root_done"], k)
                seq(dve.reciprocal(r[:], r[:]))
                seq(dve.tensor_tensor(t[:], r[:], r[:], ALU.mult))
                seq(dve.tensor_tensor(t[:], t[:], v[:], ALU.mult))
                seq(dve.tensor_scalar(t[:], t[:], -0.5, 1.5, ALU.mult, ALU.add))
                seq(dve.tensor_tensor(r[:], r[:], t[:], ALU.mult))

            def group(g, first=False, last=False):
                c0, a0 = C_FF + C_GROUP * g, A_FF + A_GROUP * g

                def up(i, first=False):
                    for s in range(2):
                        j = 2 * i + s
                        if not (first and s == 0):
                            lo(c0 + j + 1, 1 - s)
                        dve.wait_ge(S["acc_ready"], a0 + j + 1)
                        dve.scalar_tensor_tensor(out=halves(ff[s][:]), in0=acc(s), scalar=0.0, in1=halves(rB[:]),
                                                 op0=ALU.max, op1=ALU.mult).then_inc(S["acc_free"], 1)
                        dve.wait_ge(S["acc_free"], a0 + j + 1)
                        dve.tensor_tensor(ff2[s][:], ff[s][:], ff[s][:], ALU.mult).then_inc(S["ff_squared"], 1)
                        dve.wait_ge(S["ff_squared"], GK * g + j + 1)
                        dve.wait_ge(S["ff_high"], GK * g + j + 1)
                        dve.tensor_tensor(F_lo[:, bass.ds(j, 1), :].rearrange("p k n -> p (k n)"), ff2[s][:],
                                          F_hi[:, bass.ds(j, 1), :].rearrange("p k n -> p (k n)").bitcast(F32),
                                          ALU.subtract).then_inc(S["ff_ready"], 1)

                up(0, first)
                with dve.Fori(1, UP_PAIRS) as i:
                    up(i)

                def down(i, last):
                    for s in range(2):
                        if not (last and s == 1):
                            lo(c0 + GK + 2 * i + s + 1, 1 - s)
                        for e in range(2):
                            m = 4 * i + 2 * s + e
                            dve.wait_ge(S["acc_ready"], a0 + GK + m + 1)
                            tile_ = x2T[:, bass.ds(m, 1), :].rearrange("p m (h n) -> p (m h) n", h=2)
                            dve.tensor_tensor(tile_, acc(e), tile_, ALU.add).then_inc(S["acc_free"], 1)

                with dve.Fori(0, DOWN_PAIRS - 1) as i:
                    down(i, False)
                down(DOWN_PAIRS - 1, last)

            lo(C_FF + 1, 1)
            inverse_root(1, rB, tB, ff[0])
            group(0, first=True)
            with dve.Fori(1, FFG - 1) as g:
                group(g)
            group(FFG - 1, last=True)
            dve.wait_ge(S["sq_used"], 2 * KT)
            dve.tensor_scalar(halves(tF[:]), acc(2), 1.0 / D, EPS, ALU.mult, ALU.add).then_inc(S["root_in"], 1)
            inverse_root(2, rF, tF, yT[0])

            def y_quad(i, first=False):
                for s in range(4):
                    if not first:
                        dve.wait_ge(S["y_turned"], 4 * i + s - 3)
                    dve.scalar_tensor_tensor(out=yT[s][:].unsqueeze(1), in0=x2T[:, bass.ds(4 * i + s, 1), :],
                                             scalar=gfin[:, bass.ds(4 * i + s, 1)], in1=rF[:].unsqueeze(1),
                                             op0=ALU.mult, op1=ALU.mult).then_inc(S["yT_scaled"], 1)

            y_quad(0, first=True)
            with dve.Fori(1, 4) as i:
                y_quad(i)

        @block.tensor
        def _(pe):
            def product(w_slot, mhi, mlo, dst, ks, wk=0, first=True, last=True, width=P, col=0, ready=None, base=0):
                for j, k in enumerate(ks):
                    cut = slice((wk + j) * width + col, (wk + j) * width + col + P)
                    if ready is not None:
                        pe.wait_ge(S[ready], base + k + 1)
                    wh, wl = w_hi[w_slot][:, cut], w_lo[w_slot][:, cut]
                    for a, (w, x) in enumerate(((wh, mhi), (wh, mlo), (wl, mhi))):
                        for h in range(2):
                            ins = pe.matmul(dst[:, h, :], w, x[:, k, HALF * h:HALF * h + HALF],
                                            start=first and j == 0 and a == 0,
                                            stop=last and j == len(ks) - 1 and a == 2)
                return ins

            def tile(n, a, s):
                pe.wait_ge(S["split_lo"], n + 1)
                pe.wait_ge(S["acc_free"], a - 1)
                product(s, A_hi, A_lo, acc(s), range(KT)).then_inc(S["acc_ready"], 1)

            pe.wait_ge(S["consts_ready"], 1)
            pe.wait_ge(S["state_loaded"], 16)
            for m in range(8):
                ins = pe.transpose(PS[:, 4 + m // 4, 120 * (m % 4):120 * (m % 4) + 120], stN[:, m * P:(m + 1) * P],
                                   ident[0:120, 0:120])
            ins.then_inc(S["st_ready"], 1)
            pe.wait_ge(S["x_scaled"], TT)
            for k in range(KT):
                if k >= 3:
                    pe.wait_ge(S["acc_free"], k - 2)
                for t in range(TT):
                    rows = P if t < 4 else NS
                    ins = pe.transpose(x_slot(k)[:, t * P:t * P + rows], xn[0:rows, t, k * P:(k + 1) * P],
                                       ident[0:rows, 0:rows])
                ins.then_inc(S["acc_ready"], 1)
            pe.wait_ge(S["acc_free"], KT)
            with pe.Fori(0, 4) as i:
                for s in range(2):
                    tile(C_U + 2 * i + s, A_U + 2 * i + s, s)
            pe.wait_ge(S["acc_free"], A_KV)
            pe.wait_ge(S["st_copied"], 1)
            for m in range(8):
                ins = pe.transpose(PS[0:79, 4 + 2 * (m // 4), P * (m % 4):P * (m % 4) + P], uT[:, m, SEQ - PSTATE:TOK], ident[:])
            ins.then_inc(S["tail_ready"], 1)
            with pe.Fori(0, 6) as i:
                for s in range(2):
                    tile(C_KV + 2 * i + s, A_KV + 2 * i + s, s)
                for s in range(2):
                    pe.wait_ge(S["acc_free"], A_KV + 2 * i + s + 1)
                    pe.wait_ge(S[f"zn_done{s}"], 2 * i + 1)
                    for t in range(TT):
                        rows = P if t < 4 else NS
                        ins = pe.transpose(flat(2 + s)[0:rows, t * P:(t + 1) * P], zT[s][:, t * P:t * P + rows], ident[:])
                    ins.then_inc(S[f"nat_ready{s}"], 1)
            pe.wait_ge(S["split_lo"], C_NG + 1)
            for s in range(2):
                pe.wait_ge(S[f"zn_done{s}"], 13)
            product(0, A_hi, A_lo, acc(3), range(KT)).then_inc(S["ng_ready"], 1)
            pe.wait_ge(S["split_lo"], C_PM + 1)
            pe.wait_ge(S["d_ready"], 1)
            for m in range(8):
                g = m // 2
                pe.wait_ge(S["acc_free"], A_PM + m - 1)
                product(1, D_hi, D_lo, acc(m % 2), (2 * g, 2 * g + 1), wk=2 * g, width=256, col=P * (m % 2))\
                    .then_inc(S["acc_ready"], 1)
            def hidden(kv):
                pe.wait_ge(S["crow_loaded"], 288 * kv + 288)
                if kv:
                    pe.wait_ge(S["gelu_done"], 2)
                rows = crow[:].rearrange("p t h e -> p (t h) e")
                for q in range(4):
                    c = 4 * kv + q
                    pe.wait_ge(S[f"w1_loaded{c % 2}"], 32 * (c // 2) + 32)
                    for d in range(16):
                        for half in range(2):
                            n = 81 if half == 0 else 80
                            ins = pe.matmul(PS[:, 4 + half, 0:n], w1[c % 2][64 * half:64 * half + 64, d, :],
                                            rows[64 * half:64 * half + 64, 0:n, 16 * q + d],
                                            start=q == 0 and d == 0, stop=q == 3 and d == 15)
                    ins.then_inc(S["w1_used"], 1)

            def q_pair(i):
                for s in range(2):
                    tile(C_Q + 2 * i + s, A_Q + 2 * i + s, s)

            q_pair(0)
            pe.wait_ge(S["gateT_done"], 1)
            for t in range(TT):
                rows = P if t < 4 else NS
                ins = pe.transpose(PS[0:rows, 6, 48 * t:48 * t + 48], gateT[:, t * P:t * P + rows], ident[0:48, 0:48])
            ins.then_inc(S["ng_turned"], 1)
            q_pair(1)
            hidden(0)
            q_pair(2)
            pe.wait_ge(S["w2_loaded"], 32)
            pe.wait_ge(S["gelu_done"], 2)
            pe.wait_ge(S["gates_done"], 1)
            pe.matmul(PS[0:HD, 6, 0:160], w2[0][:], G[:].rearrange("p h t g -> p (h t g)"), start=True, stop=True)\
                .then_inc(S["c2_ready"], 1)
            q_pair(3)
            hidden(1)
            pe.wait_ge(S["gelu_done"], 4)
            pe.wait_ge(S["c2_done"], 1)
            for h in range(NKV):
                ins = pe.matmul(PS[0:40, 6, HD * h:HD * h + HD], G[:, h].rearrange("p t g -> p (t g)"), w2[1][:],
                                start=True, stop=True)
            ins.then_inc(S["c2_ready"], 1)
            pe.wait_ge(S["c2_done"], 2)

            def gate_part(i, m, k0, n):
                s = m % 2
                if k0 == 0:
                    pe.wait_ge(S["split_lo"], C_MG + 4 * i + m + 1)
                    pe.wait_ge(S["acc_free"], A_MG + 4 * i + m - 1)
                ins = product(s, A_hi, A_lo, acc(s), range(k0, k0 + n), wk=k0, first=k0 == 0, last=k0 + n == KT)
                if k0 + n == KT:
                    ins.then_inc(S["acc_ready"], 1)

            def sample(b, first=False):
                if first:
                    gate_part(b, 0, 0, KT)
                pe.wait_ge(S["smp_loaded"], 16 * SMP_DMAS * b + 16 * SMP_DMAS)
                for r in range(2):
                    for c in range(2):
                        for g in range(PAGES):
                            ins = pe.transpose(PS[:, 4 + r, 256 * c + P * g:256 * c + P * g + P],
                                               kvp[:, r, g, P * c:P * c + P], ident[:])
                ins.then_inc(S["KT_ready"], 1)
                if not first:
                    gate_part(b, 0, 0, 3)
                pe.wait_ge(S["KT_copied"], b + 1)
                for r in range(2):
                    for h in range(NKV):
                        c = h // 2
                        pe.matmul(PS[32 * h:32 * h + 32, 4 + r, 0:KEYS], qz[:, h].rearrange("p g t -> p (g t)"),
                                  KTs[:, r, c, :], start=True, stop=True)
                for h in range(NKV):
                    c = h // 2
                    ins = pe.matmul(PS[32 * h:32 * h + 32, 6, 0:4], qz[:, h].rearrange("p g t -> p (g t)"),
                                    kc4[:, c, :], start=True, stop=True)
                ins.then_inc(S["ss_ready"], 1)
                if not first:
                    gate_part(b, 0, 3, 10)
                for r in range(2):
                    pe.wait_ge(S["sP_ready"], 2 * b + r + 1)
                    if r == 0:
                        pe.transpose(PS[0:4, 6, 384:512], pc4[:], ident[:])
                    else:
                        pe.wait_ge(S["sPT_copied"], 2 * b + 1)
                    pe.transpose(PS[0:NT, 6, 256:384], Ps[:, r, PAST:], ident[:])
                    for g in range(PAGES):
                        ins = pe.transpose(PS[:, 6, P * g:P * g + P], Ps[:, r, P * g:P * g + P], ident[:])
                    ins.then_inc(S["sPT_ready"], 1)
                if not first:
                    gate_part(b, 0, 13, 3)
                pe.wait_ge(S["sPT_copied"], 2 * b + 2)
                pe.wait_ge(S["bank7_free"], 2 * b + 1)
                for h in range(NKV):
                    for e in range(2):
                        def mine(pT):
                            return pT[:, 32 * h:32 * h + 32].rearrange("p (k e t) -> p k e t", e=2, t=NT)[:, :, e, :]

                        out = PS[64 * e:64 * e + 64, 7, 16 * h:16 * h + 16].rearrange("p (k t) -> p k t", t=NT)
                        pe.matmul(out, vc4[:, h, :], mine(pcT4[:]), start=True, stop=False, skip_group_check=True)
                        for r in range(2):
                            for g in range(PAGES):
                                pe.matmul(out, kvp[:, r, g, 256 + HD * h:256 + HD * h + HD], mine(PTb[r][:, P * g:P * g + P]),
                                          start=False, stop=False, skip_group_check=True)
                            ins = pe.matmul(out, vnew[:, r, HD * h:HD * h + HD], mine(PTb[r][0:NT, 256:384]),
                                            start=False, stop=r == 1, skip_group_check=True)
                ins.then_inc(S["so_ready"], 1)

            def head(i, par):
                def scores(t):
                    if par == 0 and t == 0:
                        pe.wait_ge(S["sexp_done"], 3 * i + 3)
                    else:
                        pe.wait_ge(S["exp_done"], 16 * i + 8 * par + 2 * t)
                    n = P * (t + 1)
                    for r in range(2):
                        pe.matmul(PS[:, 4 + r, P * t:n], identb[:], cmask[:], start=True, stop=False)
                        ins = pe.matmul(PS[:, 4 + r, P * t:n], qh[:, par, P * t:n], KTp[:, r, P * t:n], start=False, stop=True)
                        if t:
                            ins = pe.matmul(PS[:, 4 + r, 0:P * t], qh[:, par, P * t:n], KTp[:, r, 0:P * t],
                                            start=True, stop=True)
                    ins.then_inc(S["s_ready"], 1)

                def turn(k):
                    t, r = k // 2, k % 2
                    pe.wait_ge(S["P_ready"], 16 * i + 8 * par + k + 1)
                    if k:
                        pe.wait_ge(S["PT_copied"], 16 * i + 8 * par + k)
                    else:
                        pe.wait_ge(S["cPT_copied"], 2 * i + par + 1)
                    for j in range(t + 1):
                        ins = pe.transpose(PS[:, 6, P * j:P * j + P], Pb[t % 2][:, r, P * j:P * j + P], ident[:])
                    ins.then_inc(S["PT_ready"], 1)

                def values(k):
                    t, r = k // 2, k % 2
                    pe.wait_ge(S["PT_copied"], 16 * i + 8 * par + k + 1)
                    for j in range(t + 1):
                        ins = pe.matmul(PS[64 * par:64 * par + 64, 7, P * t:P * t + P], Vp[:, r, j, :],
                                        PTb[k % 2][:, P * j:P * j + P], start=False, stop=k == 7 and j == t)
                    ins.then_inc(S["pv_done"], 1)

                def between(p):
                    u = 24 * par + 2 * p
                    gate_part(i, 1 + u // KT, u % KT, 2)

                if par:
                    pe.wait_ge(S["PT_copied"], 16 * i + 8)
                for t in range(4):
                    ins = pe.matmul(PS[:, 6, 8 * t:8 * t + 8], qh[:, par, P * t:P * t + P], kch[:], start=True, stop=True)
                ins.then_inc(S["cs_ready"], 1)
                scores(0)
                between(0)
                between(1)
                pe.wait_ge(S["cP_ready"], 2 * i + par + 1)
                for t in range(4):
                    ins = pe.transpose(PS[0:8, 6, P * t:P * t + P], pcm[:, t, :], ident[:])
                ins.then_inc(S["cPT_ready"], 1)
                scores(1)
                between(2)
                turn(0)
                pe.wait_ge(S["bank7_free"], 2 * i + 2)
                pe.matmul(PS[64 * par:64 * par + 64, 7, :], vch[:], pcT[:], start=True, stop=False)
                between(3)
                for k in range(8):
                    if k < 7:
                        turn(k + 1)
                    if k in (0, 2):
                        scores(k // 2 + 2)
                    between(4 + k)
                    values(k)

            pe.wait_ge(S["masks_ready"], 1)

            def attention(i, first=False):
                sample(i, first)
                pe.wait_ge(S["head_loaded"], 16 * HEAD_DMAS * i + 16 * HEAD_DMAS)
                head(i, 0)
                head(i, 1)

            attention(0, first=True)
            with pe.Fori(1, NB) as i:
                attention(i)

            pe.wait_ge(S["acc_free"], A_BR)
            pe.wait_ge(S["bank7_free"], 2 * NB + 1)
            with pe.Fori(0, 8) as i:
                for s in range(2):
                    pe.wait_ge(S["split_lo"], C_BR + 2 * i + s + 1)
                    pe.wait_ge(S["acc_free"], A_BR + 2 * i + s - 1)
                    product(s, A_hi, A_lo, acc(s, 4)[:, 0:2, :], range(8), ready="A_split")
                    product(s, A_hi, A_lo, acc(s, 4)[:, 2:4, :], range(8, KT), wk=8, ready="A_split").then_inc(S["acc_ready"], 1)

            def square_sums(t, k, dst, first=False, last=False):
                pe.wait_ge(S["sq_ready"], t + 1)
                for h in range(2):
                    ins = pe.matmul(dst[:, h, :], onesm[:], halves(sq[k][:])[:, h, :], start=first, stop=last)
                ins.then_inc(S["sq_used"], 1)

            def wo_pair(i, first=False):
                for s in range(2):
                    j = 2 * i + s
                    pe.wait_ge(S["split_lo"], C_WO + j + 1)
                    pe.wait_ge(S["acc_free"], A_WO + j - 1)
                    product(s, B_hi, B_lo, acc(s), range(KT), ready="merged").then_inc(S["acc_ready"], 1)
                    pe.wait_ge(S[f"xr_loaded{s}"], 32 * i + 32)
                    if first and s == 0:
                        pe.wait_ge(S["acc_free"], A_WO)
                    else:
                        pe.wait_ge(S["xT_copied"], j)
                    for t in range(TT):
                        rows = P if t < 4 else NS
                        for h in range(2):
                            a, b = max(P * t, HALF * h), min(P * t + rows, HALF * h + HALF)
                            if a < b:
                                ins = pe.matmul(acc(2)[:, h, a - HALF * h:b - HALF * h], xr[s][0:rows, t, :],
                                                ident[0:rows, a - P * t:b - P * t], start=True, stop=True)
                    ins.then_inc(S["x_turned"], 1)
                    if not (first and s == 0):
                        square_sums(j - 1, 1 - s, acc(3), first=first)

            wo_pair(0, first=True)
            with pe.Fori(1, 8) as i:
                wo_pair(i)
            square_sums(KT - 1, 1, acc(3), last=True)

            def group(g, last=False):
                c0, a0 = C_FF + C_GROUP * g, A_FF + A_GROUP * g
                with pe.Fori(0, UP_PAIRS) as i:
                    for s in range(2):
                        pe.wait_ge(S["split_lo"], c0 + 2 * i + s + 1)
                        pe.wait_ge(S["acc_free"], a0 + 2 * i + s - 1)
                        product(s, B_hi, B_lo, acc(s), range(KT), ready="h_ready").then_inc(S["acc_ready"], 1)

                def down(i, sums=False):
                    for s in range(2):
                        pe.wait_ge(S["split_lo"], c0 + GK + 2 * i + s + 1)
                        for e in range(2):
                            m = 4 * i + 2 * s + e
                            pe.wait_ge(S["acc_free"], a0 + GK + m - 1)
                            product(s, F_hi, F_lo, acc(e), range(GK), width=256, col=P * e, ready="ff_ready", base=GK * g)\
                                .then_inc(S["acc_ready"], 1)
                            if sums and m >= 2:
                                square_sums(KT + m - 2, e, acc(2), first=m == 2)

                if last:
                    for i in range(DOWN_PAIRS):
                        down(i, sums=True)
                    for e in range(2):
                        square_sums(KT + KT - 2 + e, e, acc(2), last=e == 1)
                else:
                    with pe.Fori(0, DOWN_PAIRS) as i:
                        down(i)

            with pe.Fori(0, FFG - 1) as g:
                group(g)
            group(FFG - 1, last=True)

            def y_quad(i, first=False):
                for s in range(4):
                    pe.wait_ge(S["yT_scaled"], 4 * i + s + 1)
                    if not first:
                        pe.wait_ge(S["yn_done"], 8 * i + 2 * s - 6)
                    for t in range(TT):
                        rows = P if t < 4 else NS
                        ins = pe.transpose(flat(s)[0:rows, t * P:(t + 1) * P], yT[s][:, t * P:t * P + rows], ident[:])
                    ins.then_inc(S["y_turned"], 1)

            y_quad(0, first=True)
            with pe.Fori(1, 4) as i:
                y_quad(i)


_INS = ['x_prompt', 'x_sample', 'cache_cmp_kv', 'cache_sel_kv', 'cache_win_kv', 'state_pool', 'page_table',
        'g_mix', 'w_in', 'pe_ck', 'w_ck1', 'w_ck2', 'pe_cv', 'w_cv1', 'w_cv2', 'w_pool_grp', 'pool_scale',
        'w_br_nsa', 'w_br_pool', 'w_o', 'g_mlp', 'w_up', 'w_down', 'g_final']
_OUTS = [(1, SEQ, D), (NB, NT, D), (1, 1, SEQ, 2, NKV, HD), (1, 1, SEQ, 2, NKV, HD), (1, 1, SEQ, 2, NKV, HD),
         (1, 1, PSTATE, PW), (1, NB, NT, 2, NKV, HD), (1, NB, NT, 2, NKV, HD), (1, NB, KEYS, 2, NKV, HD),
         (1, NB, PSTATE, PW)]


def kernel(**inputs):
    import numpy as _np
    import concourse.bacc as _bacc
    from concourse import mybir as _mybir
    from concourse.bass_utils import run_bass_kernel_spmd as _run

    nc = _bacc.Bacc("TRN2", target_bir_lowering=False, num_devices=1)
    arrays, args = {}, []
    for name in _INS:
        a = _np.ascontiguousarray(inputs[name])
        arrays[f"in_{name}_dram"] = a
        args.append(nc.dram_tensor(f"in_{name}_dram", a.shape, _mybir.dt.from_np(a.dtype), kind="ExternalInput").ap())
    for i, shape in enumerate(_OUTS):
        args.append(nc.dram_tensor(f"out_{i}_dram", shape, F32, kind="ExternalOutput").ap())
    build(nc, *args)
    r = _run(nc, [arrays], core_ids=[0])
    return tuple(r.results[0][f"out_{i}_dram"] for i in range(len(_OUTS)))
```
